# Optimizing a Trainium2 kernel written in Bass

```python
import math
import jax, jax.numpy as jnp
from jax import lax
import numpy as np

D_MODEL = 1024
BATCH = 1
SEQ = 512
DEPTH = 2

CHUNK = 64
EPS = 1e-6
ROPE_THETA = 10000.0

A_WIDTH = 512
A_GROUPS = 4
A_GROUP_DIM = A_WIDTH // A_GROUPS
A_BLOCK = 128

B_HEADS = 4
B_HEAD_DIM = 128
B_WIDTH = B_HEADS * B_HEAD_DIM
IDX_HEADS = 8
IDX_DIM = 64
TOPK_MAX = 256
Q_BLOCK = 128

SPLIT_SIZES = (A_WIDTH, A_WIDTH, A_WIDTH,
               B_WIDTH, B_WIDTH, B_WIDTH, B_WIDTH,
               IDX_HEADS * IDX_DIM, IDX_DIM, IDX_HEADS,
               D_MODEL, D_MODEL)
IN_WIDTH = sum(SPLIT_SIZES)

kernel_name = "hybrid_gmlp_dsa_gated_trunk"

def rms_norm(x, g):
    x32 = x.astype(jnp.float32)
    y = x32 * lax.rsqrt(jnp.mean(x32 * x32, axis=-1, keepdims=True) + EPS)
    return (y * g.astype(jnp.float32)).astype(x.dtype)

def layer_norm(x, g, b):
    x32 = x.astype(jnp.float32)
    mu = jnp.mean(x32, axis=-1, keepdims=True)
    xc = x32 - mu
    y = xc * lax.rsqrt(jnp.mean(xc * xc, axis=-1, keepdims=True) + EPS)
    return (y * g.astype(jnp.float32) + b.astype(jnp.float32)).astype(x.dtype)

def rope_tables(s, dim, dtype):
    pos = jnp.arange(s, dtype=jnp.float32)
    inv = ROPE_THETA ** (-jnp.arange(0, dim, 2, dtype=jnp.float32) / dim)
    ang = pos[:, None] * inv[None, :]
    return jnp.cos(ang).astype(dtype), jnp.sin(ang).astype(dtype)

def apply_rope(x, cos, sin):
    x1, x2 = jnp.split(x, 2, axis=-1)
    c = cos[:, None, :]
    s = sin[:, None, :]
    return jnp.concatenate([x1 * c - x2 * s, x1 * s + x2 * c], axis=-1)

def split_columns(proj):
    points = []
    acc = 0
    for size in SPLIT_SIZES[:-1]:
        acc += size
        points.append(acc)
    return jnp.split(proj, points, axis=-1)

def spatial_gating_branch(u, v, z, ws, bs, ln_g, ln_b):
    b, s, _ = u.shape
    v = layer_norm(v, ln_g, ln_b)
    chunk_id = jnp.arange(A_BLOCK) // CHUNK
    mask = chunk_id[None, :] <= chunk_id[:, None]
    w = jnp.where(mask[None], ws, jnp.zeros_like(ws))
    vb = v.reshape(b, s // A_BLOCK, A_BLOCK, A_GROUPS, A_GROUP_DIM)
    mixed = jnp.einsum('gij,bnjgc->bnigc', w, vb) + bs.T[:, :, None]
    return u * mixed.reshape(b, s, A_WIDTH) * jax.nn.silu(z)

def sparse_attention_branch(q, k, v, qi, ki, wi, topk):
    b, s, h, dh = q.shape
    nb = s // Q_BLOCK
    key_chunk = jnp.arange(s) // CHUNK
    ki32 = ki.astype(jnp.float32)
    gather = jax.vmap(lambda arr, ix: arr[ix])
    att_scale = B_HEAD_DIM ** -0.5
    idx_scale = (IDX_DIM ** -0.5) * (IDX_HEADS ** -0.5)

    def block(args):
        n, qb, qib, wib = args
        q_chunk = (n * Q_BLOCK + jnp.arange(Q_BLOCK)) // CHUNK
        admissible = key_chunk[None, :] <= q_chunk[:, None]
        logits = jnp.einsum('bqhd,bsd->bqhs', qib.astype(jnp.float32), ki32)
        score = jnp.einsum('bqh,bqhs->bqs', wib.astype(jnp.float32), jax.nn.relu(logits)) * idx_scale
        score = jnp.where(admissible[None], score, -jnp.inf)
        _, idx = lax.top_k(score, topk)
        valid = key_chunk[idx] <= q_chunk[None, :, None]
        kg = gather(k, idx)
        vg = gather(v, idx)
        att = jnp.einsum('bqhd,bqkhd->bqhk', qb, kg).astype(jnp.float32) * att_scale
        att = jnp.where(valid[:, :, None, :], att, -jnp.inf)
        p = jax.nn.softmax(att, axis=-1).astype(v.dtype)
        return jnp.einsum('bqhk,bqkhd->bqhd', p, vg)

    to_blocks = lambda t: jnp.moveaxis(t.reshape((b, nb, Q_BLOCK) + t.shape[2:]), 1, 0)
    out = lax.map(block, (jnp.arange(nb), to_blocks(q), to_blocks(qi), to_blocks(wi)))
    return jnp.moveaxis(out, 0, 1).reshape(b, s, h * dh)

def setup_inputs(seed: int = 0) -> dict:
    key = jax.random.key(seed)
    ks = jax.random.split(key, 16)
    f32 = jnp.float32
    nrm = lambda k, shape, scale: jax.random.normal(k, shape, f32) * scale
    return {
        "x": jax.random.normal(ks[0], (BATCH, SEQ, D_MODEL), f32),
        "norm_g": 1.0 + nrm(ks[1], (DEPTH, D_MODEL), 0.02),
        "w_in": nrm(ks[2], (DEPTH, D_MODEL, IN_WIDTH), D_MODEL ** -0.5),
        "gate_b": nrm(ks[3], (DEPTH, 2, D_MODEL), 0.02),
        "a_ln_g": 1.0 + nrm(ks[4], (DEPTH, A_WIDTH), 0.02),
        "a_ln_b": nrm(ks[5], (DEPTH, A_WIDTH), 0.02),
        "a_ws": nrm(ks[6], (DEPTH, A_GROUPS, A_BLOCK, A_BLOCK), A_BLOCK ** -0.5),
        "a_bs": 1.0 + nrm(ks[7], (DEPTH, A_GROUPS, A_BLOCK), 0.02),
        "q_norm_g": 1.0 + nrm(ks[8], (DEPTH, B_HEAD_DIM), 0.02),
        "k_norm_g": 1.0 + nrm(ks[9], (DEPTH, B_HEAD_DIM), 0.02),
        "w_oa": nrm(ks[10], (DEPTH, A_WIDTH, D_MODEL), A_WIDTH ** -0.5),
        "w_ob": nrm(ks[11], (DEPTH, B_WIDTH, D_MODEL), B_WIDTH ** -0.5),
        "w_out": nrm(ks[12], (DEPTH, D_MODEL, D_MODEL), D_MODEL ** -0.5),
    }

def reference(x, norm_g, w_in, gate_b, a_ln_g, a_ln_b, a_ws, a_bs, q_norm_g, k_norm_g,
              w_oa, w_ob, w_out):
    b, s, _ = x.shape
    topk = min(TOPK_MAX, s // 4)
    cos_q, sin_q = rope_tables(s, B_HEAD_DIM, x.dtype)
    cos_i, sin_i = rope_tables(s, IDX_DIM, x.dtype)
    for l in range(DEPTH):
        h = rms_norm(x, norm_g[l])
        proj = jnp.einsum('bsd,de->bse', h, w_in[l])
        (a_u, a_v, a_z, b_q, b_k, b_v, b_z, i_q, i_k, i_w, g_a, g_b) = split_columns(proj)

        y_a = spatial_gating_branch(jax.nn.gelu(a_u), jax.nn.gelu(a_v), a_z,
                                    a_ws[l], a_bs[l], a_ln_g[l], a_ln_b[l])

        q = apply_rope(rms_norm(b_q.reshape(b, s, B_HEADS, B_HEAD_DIM), q_norm_g[l]), cos_q, sin_q)
        k = apply_rope(rms_norm(b_k.reshape(b, s, B_HEADS, B_HEAD_DIM), k_norm_g[l]), cos_q, sin_q)
        v = b_v.reshape(b, s, B_HEADS, B_HEAD_DIM)
        qi = apply_rope(i_q.reshape(b, s, IDX_HEADS, IDX_DIM), cos_i, sin_i)
        ki = apply_rope(i_k[:, :, None, :], cos_i, sin_i)[:, :, 0, :]
        att = sparse_attention_branch(q, k, v, qi, ki, i_w, topk)
        y_b = att * jax.nn.silu(b_z)

        o_a = jnp.einsum('bse,ed->bsd', y_a, w_oa[l])
        o_b = jnp.einsum('bse,ed->bsd', y_b, w_ob[l])
        merged = jax.nn.sigmoid(g_a + gate_b[l, 0]) * o_a + jax.nn.sigmoid(g_b + gate_b[l, 1]) * o_b
        x = x + jnp.einsum('bsd,de->bse', merged, w_out[l])
    return x


_drawn_inputs = setup_inputs


def setup_inputs(seed=0):
    import zlib

    import numpy as np

    out = dict(_drawn_inputs(seed))
    spreads = {}
    factors = {'norm_g': 3.473,
     'gate_b': 8.0,
     'a_ln_g': 8.0,
     'a_ln_b': 8.0,
     'a_bs': 8.0,
     'q_norm_g': 8.0,
     'k_norm_g': 8.0}
    for name, (base, spread) in spreads.items():
        noise = np.random.default_rng([zlib.crc32(name.encode()), seed]).standard_normal(out[name].shape)
        drawn = base * np.exp(spread * noise) if base else spread * noise
        out[name] = __import__('jax').numpy.asarray(drawn.astype(out[name].dtype))
    for name, factor in factors.items():
        out[name] = (out[name] * factor).astype(out[name].dtype)
    return out
```

```python
from contextlib import ExitStack

import concourse.bass as bass
import numpy as np
from concourse import mybir
from concourse.alu_op_type import AluOpType as ALU

F32 = mybir.dt.float32
F32R = mybir.dt.float32r
ACT = mybir.ActivationFunctionType
AX = mybir.AxisListType

P = 128
DEPTH, SEQ, D = 2, 512, 1024
CHUNK = 64
EPS = 1e-6
ROPE_THETA = 10000.0
A_WIDTH, A_GROUPS = 512, 4
HEADS, DH = 4, 128
IH, ID = 8, 64
TOPK = min(256, SEQ // 4)
SPLITS = dict(u=A_WIDTH, va=A_WIDTH, za=A_WIDTH, q=HEADS * DH, k=HEADS * DH, vb=HEADS * DH, zb=HEADS * DH,
              iq=IH * ID, ik=ID, iw=IH, ga=D, gb=D)
COL = dict(zip(SPLITS, np.cumsum([0] + list(SPLITS.values())[:-1]).tolist()))
IN_WIDTH = sum(SPLITS.values())

TILES = SEQ // P
KD = D // P
W512 = 512
SMALL = ID + IH
ROT_I = (IH + 1) * ID
ATT_SCALE = DH ** -0.5
IDX_SCALE = ID ** -0.5 * IH ** -0.5
FILL = -(2.0 ** 126)
TAKEN = -(2.0 ** 127)
SILU_HALF = 0.5

GROUPS = [
    ("iq", "w_in", COL["iq"], 4), ("k", "w_in", COL["k"], 4), ("q", "w_in", COL["q"], 4),
    ("vb", "w_in", COL["vb"], 4), ("va", "w_in", COL["va"], 4), ("u", "w_in", COL["u"], 4),
    ("zb", "w_in", COL["zb"], 4), ("za", "w_in", COL["za"], 4),
    ("ga", "w_in", COL["ga"], 4), ("ga", "w_in", COL["ga"] + W512, 4),
    ("oa", "w_oa", 0, 8),
    ("gb", "w_in", COL["gb"], 4), ("gb", "w_in", COL["gb"] + W512, 4),
    ("ob", "w_ob", 0, 8),
    ("out", "w_out", 0, 4), ("out", "w_out", W512, 4),
]
TOKEN_MAJOR = {"iq", "k", "q", "vb", "va", "out"}
FIRST_JOB = np.cumsum([0] + [g[3] for g in GROUPS]).tolist()
NJOBS = FIRST_JOB[-1]
NQ = 4
RAW = 4
GBANKS = 3
assert NJOBS % GBANKS == 0 and (len(GROUPS) * NQ) % RAW == 0


def jobs_of(name):
    return [FIRST_JOB[g] + j for g in range(len(GROUPS)) if GROUPS[g][0] == name for j in range(GROUPS[g][3])]


JOB_IQ, JOB_K, JOB_Q, JOB_VB, JOB_VA, JOB_U, JOB_ZB, JOB_ZA, JOB_GA, JOB_OA, JOB_GB, JOB_OB, JOB_OUT = (
    jobs_of(n) for n in ("iq", "k", "q", "vb", "va", "u", "zb", "za", "ga", "oa", "gb", "ob", "out"))

AFTER_QI = {JOB_IQ[t] + 2: t for t in range(TILES)}
AFTER_K = {JOB_K[t] + 2: t for t in range(TILES)}
AFTER_Q = {JOB_Q[t] + 2: t for t in range(TILES)}
IDX_STEPS = [(b, h) for b in range(1, TILES) for h in range(IH)]
AFTER_IDX = {6 + n // 2: [n - n % 2, n - n % 2 + 1] for n in range(len(IDX_STEPS))}
AFTER_WS = JOB_VA[2]
AFTER_MIX = {JOB_ZB[2]: [0, 1], JOB_ZB[3]: [2, 3]}
ATT_STEPS = [(h, b) for h in range(HEADS) for b in range(TILES)]
_slots = list(range(JOB_ZA[2], JOB_GA[-1] + 1)) + JOB_OA[1::2] + JOB_GB
AFTER_ATT = {_slots[i]: i for i in range(len(ATT_STEPS) + 2)}
ROUNDS = TOPK // 8
TOPK_SLOTS = ([(s, 1, 4) for s in range(10, 14)] + [(s, 2, 3) for s in range(14, 20)]
              + [(s, 3, 2) for s in range(20, 28)])


class Signal:

    def __init__(self, ctx, nc, name, per_layer, seeded=True):
        self.sem, self.per = ctx.enter_context(nc.semaphore(name)), per_layer
        self.seeded = seeded

    def at(self, layer, n):
        return layer * self.per + (self.per if self.seeded else 0) + n


class Steps:

    def __init__(self, ctx, nc, name):
        self.sem, self.n, self.waited = ctx.enter_context(nc.semaphore(name)), 0, 0

    def link(self, engine, instruction):
        self.mark(instruction)
        self.join(engine)

    def mark(self, instruction):
        self.n += 1
        instruction.then_inc(self.sem, 1)

    def join(self, engine):
        if self.n > self.waited:
            engine.wait_ge(self.sem, self.n)
            self.waited = self.n

    def end_layer(self, engine):
        self.join(engine)
        engine.sem_clear(self.sem)
        self.n = self.waited = 0


def trunk(nc, x, norm_g, w_in, gate_b, a_ln_g, a_ln_b, a_ws, a_bs, q_norm_g, k_norm_g, w_oa, w_ob, w_out,
          ident, cos_qk, sin_qk, cos_i, sin_i, out):
    ctx = ExitStack()
    with ctx:
        def sb(name, shape, dt=F32, keep=ctx):
            return keep.enter_context(nc.sbuf_tensor(name, shape, dt))

        w_hi = sb("w_hi", [P, 2, KD, W512], F32R)
        w_lo = sb("w_lo", [P, 2, KD, W512], F32R)
        w_raw = sb("w_raw", [P, RAW, 2, W512])
        h_hi = sb("h_hi", [P, KD, SEQ], F32R)
        h_lo = sb("h_lo", [P, KD, SEQ], F32R)
        with ExitStack() as early:
            xn = sb("xn", [P, 2, D], keep=early)
        with ExitStack() as early:
            k_t = sb("k_t", [P, HEADS, SEQ], keep=early)
            q_t = sb("q_t", [P, HEADS, SEQ], keep=early)
        yb_hi = sb("yb_hi", [P, HEADS, SEQ], F32R)
        yb_lo = sb("yb_lo", [P, HEADS, SEQ], F32R)
        with ExitStack() as early:
            x_sb = sb("x_sb", [P, TILES, D], keep=early)
        v_b = sb("v_b", [P, TILES, HEADS * DH])
        with ExitStack() as early:
            qi_t = sb("qi_t", [P, IH // 2, SEQ - P], keep=early)
            ki_t = sb("ki_t", [P, SEQ], keep=early)
        z_b = sb("z_b", [P, HEADS, SEQ])
        with ExitStack() as early:
            v_a = sb("v_a", [P, TILES, A_WIDTH], keep=early)
            u_a = sb("u_a", [P, A_GROUPS, SEQ], keep=early)
        with ExitStack() as early:
            s_raw = sb("s_raw", [P, KD, SMALL], keep=early)
            s_hi = sb("s_hi", [P, KD, SMALL], F32R, keep=early)
            s_lo = sb("s_lo", [P, KD, SMALL], F32R, keep=early)
        g_a = sb("g_a", [P, KD, SEQ])
        with ExitStack() as early:
            norm_bc = sb("norm_bc", [P, D], keep=early)
            lng_bc = sb("lng_bc", [P, A_WIDTH], keep=early)
            lnb_bc = sb("lnb_bc", [P, A_WIDTH], keep=early)
            bs_bc = sb("bs_bc", [P, A_GROUPS, P], keep=early)
            ws_raw = sb("ws_raw", [P, A_GROUPS, P], keep=early)
            ws_t = sb("ws_t", [P, A_GROUPS, P], keep=early)
            kg_bc = sb("kg_bc", [P, DH], keep=early)
            qg_bc = sb("qg_bc", [P, DH], keep=early)
        with ExitStack() as early:
            ya_hi = sb("ya_hi", [P, A_GROUPS, SEQ], F32R, keep=early)
            ya_lo = sb("ya_lo", [P, A_GROUPS, SEQ], F32R, keep=early)
        g_b = sb("g_b", [P, KD, SEQ])
        with ExitStack() as early:
            stage = sb("stage", [P, 2, ROT_I + IH], keep=early)
            rope_a = sb("rope_a", [P, ROT_I], keep=early)
            rope_b = sb("rope_b", [P, ROT_I], keep=early)
        t_half = sb("t_half", [P, 2, SEQ])
        silu_z = sb("silu_z", [P, SEQ])
        um = sb("um", [P, (2 * (ROT_I + IH) + 2 * ROT_I) - 3 * SEQ])
        rot = sb("rot", [P, ROT_I + ID])
        probs = sb("probs", [P, 2, SEQ])
        probs_t = sb("probs_t", [P, SEQ])
        score = sb("score", [P, sum(P * (b + 1) for b in range(1, TILES))])
        eye = sb("eye", [P, P])
        cq = sb("cq", [P, TILES, DH])
        sq = sb("sq", [P, TILES, DH])
        ci = sb("ci", [P, TILES, ID])
        si = sb("si", [P, TILES, ID])
        diag = sb("diag", [P, P])
        gate_raw = sb("gate_raw", [P, 2 * KD])
        gate_half = sb("gate_half", [P, 2 * KD])
        eps = sb("eps", [P, 1])
        head_w = sb("head_w", [P, TILES, IH])
        top8 = sb("top8", [P, 8])
        ms = sb("ms", [P, 2 * TILES * HEADS + TILES])
        std = sb("std", [P, 2 * TILES * HEADS + TILES])
        rstd = sb("rstd", [P, 2 * TILES * HEADS + TILES])
        bn = sb("bn", [P, TILES, 6])
        mv = sb("mv", [P, TILES, 2])
        ln_std = sb("ln_std", [P, TILES])
        ln_rstd = sb("ln_rstd", [P, TILES])
        row_max = sb("row_max", [P, len(ATT_STEPS)])
        neg_max = sb("neg_max", [P, len(ATT_STEPS)])
        row_sum = sb("row_sum", [P, len(ATT_STEPS)])
        row_inv = sb("row_inv", [P, len(ATT_STEPS)])

        bank = [ctx.enter_context(nc.psum_tensor(f"bank{i}", [P, W512], F32)) for i in range(8)]

        def sig(name, per, seeded=True):
            return Signal(ctx, nc, name, per, seeded)

        s_const = ctx.enter_context(nc.semaphore("constants_in"))
        s_x0 = ctx.enter_context(nc.semaphore("x_in"))
        s_par = sig("parameters_in", 16 * 9, False)
        s_wraw = [sig(f"weights_raw{i}", 16 * len(GROUPS) * NQ // RAW, False) for i in range(RAW)]
        s_whi = sig("weights_hi", len(GROUPS) * NQ)
        s_wlo = sig("weights_lo", len(GROUPS) * NQ)
        s_shi = sig("small_weights_hi", 1)
        s_slo = sig("small_weights_lo", 1)
        s_init = ctx.enter_context(nc.semaphore("tiles_initialised"))
        s_ghalf = sig("gate_bias_halved", 1)
        s_xstd = sig("x_std", TILES)
        s_xn = sig("x_normalised", TILES)
        s_xt = sig("x_transposed", 2 * TILES)
        s_hhi = sig("h_hi_written", 2 * TILES)
        s_hlo = sig("h_lo_written", 2 * TILES)
        s_job = sig("job_done", NJOBS)
        s_free = [sig(f"bank_free{i}", NJOBS // GBANKS) for i in range(GBANKS)]
        s_small = sig("small_product_copied", TILES)
        s_stage = sig("tile_staged", 3 * TILES)
        s_xg = sig("heads_scaled", 2 * TILES)
        s_rinv = sig("heads_rstd", 2 * TILES)
        s_rot = sig("tile_rotated", 3 * TILES)
        s_rott = sig("rotated_transposed", 3 * TILES)
        s_rotc = sig("rotated_copied", 3 * TILES)
        s_idxp = sig("index_logits", len(IDX_STEPS))
        s_relu = sig("index_relu", len(IDX_STEPS))
        s_idx = sig("index_added", len(IDX_STEPS))
        s_vb = sig("v_copied", TILES)
        s_va = sig("va_gelu", TILES)
        s_u = sig("u_gelu", TILES)
        s_wst = sig("ws_transposed", 1)
        s_wsc = sig("ws_copied", 1)
        s_wsz = sig("ws_masked", 1)
        s_lnv = sig("ln_variance", 1)
        s_lnstd = sig("ln_std", 1)
        s_ln = sig("ln_applied", TILES)
        s_mix = sig("mixed", A_GROUPS)
        s_um = sig("u_times_mixed", A_GROUPS)
        s_tanh = sig("tanh_half_z", 8)
        s_zused = sig("tanh_half_z_used", 8)
        s_ya = sig("ya_ready", A_GROUPS)
        s_yahi = sig("ya_hi_written", A_GROUPS)
        s_yalo = sig("ya_lo_written", A_GROUPS)
        s_ga = sig("gate_a", KD)
        s_gb = sig("gate_b", KD)
        s_ma = sig("branch_a_gated", KD)
        s_sum = sig("branches_added", KD)
        s_mhi = sig("merged_hi", KD)
        s_mlo = sig("merged_lo", KD)
        s_qk = sig("scores", len(ATT_STEPS))
        s_max = sig("score_max", len(ATT_STEPS))
        s_exp = sig("exponentials", len(ATT_STEPS))
        s_prob = sig("probs_scaled", len(ATT_STEPS))
        s_pt = sig("probs_transposed", len(ATT_STEPS))
        s_ptc = sig("probs_t_copied", len(ATT_STEPS))
        s_pv = sig("attended", len(ATT_STEPS))
        s_yb = sig("yb_ready", HEADS)
        s_ybhi = sig("yb_hi_written", HEADS)
        s_yblo = sig("yb_lo_written", HEADS)
        s_xback = sig("x_reloaded", 16, False)
        s_res = sig("residual_added", 2 * TILES)
        s_out = sig("out_stored", 16 * TILES)
        s_out0 = ctx.enter_context(nc.semaphore("x_copied_to_out"))
        vec = Steps(ctx, nc, "vector_steps")
        act_ = Steps(ctx, nc, "scalar_steps")
        poo = Steps(ctx, nc, "gpsimd_steps")

        def seed(engine, *signals):
            for s in signals:
                engine.sem_inc(s.sem, s.per)

        waits_over = ctx.enter_context(nc.semaphore("waits_over"))

        def pause(engine):
            engine.sem_inc(waits_over, 1)

        block = ctx.enter_context(nc.Block())

        def block_cols(b):
            at = sum(P * (c + 1) for c in range(1, b))
            return slice(at, at + P * (b + 1))

        def w_slot(g):
            return g % 2

        def slot_free(layer, g):
            return s_job.at(layer, FIRST_JOB[g - 1] if g >= 2 else FIRST_JOB[g - 1 + len(GROUPS)] - NJOBS)

        def quarter_in(j):
            g = next(i for i in range(len(GROUPS)) if FIRST_JOB[i] <= j < FIRST_JOB[i + 1])
            if g + 1 == len(GROUPS):
                return None
            i, wide = j - FIRST_JOB[g], GROUPS[g][3] // NQ
            return (g + 1, i // wide) if i % wide == 0 else None

        @block.sync
        def _(sp):
            for t in range(TILES):
                sp.dma_start(x_sb[:, t, :], x[t * P:(t + 1) * P, :]).then_inc(s_x0, 16)
            for dst, src in ((eye, ident), (cq, cos_qk), (sq, sin_qk), (ci, cos_i), (si, sin_i)):
                sp.dma_start(dst[:], src).then_inc(s_const, 16)
            seed(sp, s_out)
            with sp.Fori(0, DEPTH) as layer:
                for g, (name, matrix, col, _) in enumerate(GROUPS):
                    src = dict(w_in=w_in, w_oa=w_oa, w_ob=w_ob, w_out=w_out)[matrix][bass.ds(layer, 1)]
                    for qt in range(NQ):
                        n = g * NQ + qt
                        sp.wait_ge(s_wlo.sem, s_wlo.at(layer, n - RAW + 1))
                        pause(sp)
                        if matrix in ("w_oa", "w_ob"):
                            part = src[:, qt * P:(qt + 1) * P, :].rearrange("a p (c n) -> (a p) c n", c=2)
                        else:
                            part = src[:, 2 * qt * P:(2 * qt + 2) * P, col:col + W512] \
                                .rearrange("a (k p) n -> p (a k) n", p=P)
                        sp.dma_start(w_raw[:, n % RAW], part).then_inc(s_wraw[n % RAW].sem, 16)
                for t in range(TILES):
                    sp.wait_ge(s_res.sem, s_res.at(layer, TILES + t + 1))
                    sp.dma_start(out[t * P:(t + 1) * P, :], x_sb[:, t, :]).then_inc(s_out.sem, 16)
            sp.wait_ge(s_out.sem, s_out.at(DEPTH, 0))

        @block.gpsimd
        def _(pool):
            seed(pool, s_xg)
            pool.dma_start(out, x).then_inc(s_out0, 16)
            pool.wait_ge(s_out0, 16)
            with pool.Fori(0, DEPTH) as layer:
                l = bass.ds(layer, 1)
                pool.wait_ge(s_mlo.sem, s_mlo.at(layer, 0))
                pause(pool)
                for dst, src in ((norm_bc, norm_g), (kg_bc, k_norm_g), (qg_bc, q_norm_g),
                                 (lng_bc, a_ln_g), (lnb_bc, a_ln_b)):
                    pool.dma_start(dst[:], src[l].to_broadcast([P, dst.shape[1]])).then_inc(s_par.sem, 16)
                pool.dma_start(s_raw[:], w_in[l, :, COL["ik"]:COL["ik"] + SMALL]
                               .rearrange("a (k p) n -> p (a k) n", p=P)).then_inc(s_par.sem, 16)
                pool.dma_start(bs_bc[:], a_bs[l].rearrange("a (g i) -> a g i", g=A_GROUPS)
                               .to_broadcast([P, A_GROUPS, P])).then_inc(s_par.sem, 16)
                pool.dma_start(ws_raw[:], a_ws[l].rearrange("a g i j -> i (a g) j")).then_inc(s_par.sem, 16)
                pool.dma_start(gate_raw[:], gate_b[l].rearrange("a p c -> (a p) c")).then_inc(s_par.sem, 16)
                pool.wait_ge(s_par.sem, s_par.at(layer, 16 * 9))
                for n in range(2 * TILES):
                    g_bc = kg_bc if n < TILES else qg_bc
                    tile = stage[:, (TILES + n) % 2, 0:HEADS * DH].rearrange("p (h d) -> p h d", h=HEADS)
                    pool.wait_ge(s_rinv.sem, s_rinv.at(layer, n + 1))
                    poo.link(pool, nc.gpsimd.tensor_tensor(
                        tile, tile, rstd[:, HEADS * n:HEADS * n + HEADS].unsqueeze(2).to_broadcast([P, HEADS, DH]),
                        ALU.mult))
                    nc.gpsimd.tensor_tensor(tile, tile, g_bc[:].unsqueeze(1).to_broadcast([P, HEADS, DH]),
                                            ALU.mult).then_inc(s_xg.sem, 1)
                pool.wait_ge(s_yblo.sem, s_yblo.at(layer, HEADS))
                pool.wait_ge(s_out.sem, s_out.at(layer, 0))
                pause(pool)
                pool.dma_start(x_sb[:], out.rearrange("(t p) d -> p t d", p=P)).then_inc(s_xback.sem, 16)
                pause(pool)
                poo.end_layer(pool)

        @block.tensor
        def _(pe):
            seed(pe, s_job, s_xt, s_rott, s_idxp, s_wst, s_mix, s_qk, s_pt, s_pv)
            pe.wait_ge(s_const, 16 * 5)

            def transpose_x(layer, t):
                pe.wait_ge(s_xn.sem, s_xn.at(layer, t + 1))
                if t >= 2:
                    pe.wait_ge(s_hlo.sem, s_hlo.at(layer, 2 * (t - 1)))
                for half in range(2):
                    dst = bank[3 + 2 * (t % 2) + half]
                    for k in range(4):
                        kk = 4 * half + k
                        last = nc.tensor.transpose(dst[:, k * P:(k + 1) * P], xn[:, t % 2, kk * P:(kk + 1) * P], eye[:])
                    last.then_inc(s_xt.sem, 1)

            def transpose_rotated(layer, n):
                pe.wait_ge(s_rot.sem, s_rot.at(layer, n + 1))
                if n == 0:
                    pe.wait_ge(s_hlo.sem, s_hlo.at(layer, 2 * TILES))
                else:
                    pe.wait_ge(s_rotc.sem, s_rotc.at(layer, n))
                index = n < TILES
                for c in range(4 if n else 0):
                    last = nc.tensor.transpose(bank[5][:, c * P:(c + 1) * P], rot[:, c * P:(c + 1) * P], eye[:])
                if index:
                    last = nc.tensor.transpose(bank[6][:, 0:P], rot[:, IH * ID:IH * ID + 2 * ID], eye[:])
                last.then_inc(s_rott.sem, 1)

            def index_logits(layer, n):
                b, h = IDX_STEPS[n]
                if n < 2:
                    pe.wait_ge(s_rotc.sem, s_rotc.at(layer, TILES))
                else:
                    pe.wait_ge(s_relu.sem, s_relu.at(layer, n - 1))
                half = slice(ID * (h % 2), ID * (h % 2) + ID)
                nc.tensor.matmul(bank[3 + n % 2][:, 0:P * (b + 1)], qi_t[half, h // 2, (b - 1) * P:b * P],
                                 ki_t[half, 0:P * (b + 1)], start=True, stop=True).then_inc(s_idxp.sem, 1)

            def transpose_ws(layer):
                pe.wait_ge(s_par.sem, s_par.at(layer, 16 * 9))
                pe.wait_ge(s_rotc.sem, s_rotc.at(layer, 3 * TILES))
                for g in range(A_GROUPS):
                    last = nc.tensor.transpose(bank[5][:, g * P:(g + 1) * P], ws_raw[:, g], eye[:])
                last.then_inc(s_wst.sem, 1)

            def mix(layer, g):
                if g == 0:
                    pe.wait_ge(s_ln.sem, s_ln.at(layer, TILES))
                    pe.wait_ge(s_wsc.sem, s_wsc.at(layer, 1))
                    pe.wait_ge(s_wsz.sem, s_wsz.at(layer, 1))
                    pe.wait_ge(s_relu.sem, s_relu.at(layer, len(IDX_STEPS)))
                for n in range(TILES):
                    last = nc.tensor.matmul(bank[3 + g][:, n * P:(n + 1) * P], v_a[:, n, g * P:(g + 1) * P],
                                            ws_t[:, g], start=True, stop=True)
                last.then_inc(s_mix.sem, 1)

            def attend(layer, i):
                if i >= 2:
                    h, b = ATT_STEPS[i - 2]
                    pe.wait_ge(s_ptc.sem, s_ptc.at(layer, i - 1))
                    if b == 0 and h:
                        pe.wait_ge(s_yb.sem, s_yb.at(layer, h))
                    for c in range(b + 1):
                        last = nc.tensor.matmul(bank[7][:, b * P:(b + 1) * P], v_b[:, c, h * DH:(h + 1) * DH],
                                                probs_t[:, c * P:(c + 1) * P], start=(c == 0), stop=(c == b))
                    last.then_inc(s_pv.sem, 1)
                if 1 <= i <= len(ATT_STEPS):
                    h, b = ATT_STEPS[i - 1]
                    pe.wait_ge(s_prob.sem, s_prob.at(layer, i))
                    if i >= 2:
                        pe.wait_ge(s_ptc.sem, s_ptc.at(layer, i - 1))
                    for c in range(b + 1):
                        last = nc.tensor.transpose(bank[5][:, c * P:(c + 1) * P],
                                                   probs[:, (i - 1) % 2, c * P:(c + 1) * P], eye[:])
                    last.then_inc(s_pt.sem, 1)
                if i < len(ATT_STEPS):
                    h, b = ATT_STEPS[i]
                    if i == 0:
                        pe.wait_ge(s_um.sem, s_um.at(layer, A_GROUPS))
                    if i >= 2:
                        pe.wait_ge(s_max.sem, s_max.at(layer, i - 1))
                    nc.tensor.matmul(bank[3 + i % 2][:, 0:P * (b + 1)], q_t[:, h, b * P:(b + 1) * P],
                                     k_t[:, h, 0:P * (b + 1)], start=True, stop=True).then_inc(s_qk.sem, 1)

            def three_pass(dst, pairs, ready=None):
                for n, (s_h, s_l, m_h, m_l) in enumerate(pairs):
                    if ready:
                        ready(n)
                    nc.tensor.matmul(dst, s_h, m_l, start=(n == 0), stop=False)
                    nc.tensor.matmul(dst, s_l, m_h, start=False, stop=False)
                    last = nc.tensor.matmul(dst, s_h, m_h, start=False, stop=(n == len(pairs) - 1))
                return last

            def job(layer, g, j):
                name = GROUPS[g][0]
                n, i, slot = FIRST_JOB[g] + j, j, w_slot(g)
                dst = bank[n % GBANKS]
                pe.wait_ge(s_free[n % GBANKS].sem, s_free[n % GBANKS].at(layer, n // GBANKS))
                if name in ("oa", "ob"):
                    y_hi, y_lo = (ya_hi, ya_lo) if name == "oa" else (yb_hi, yb_lo)
                    done = s_yalo if name == "oa" else s_yblo
                    pairs = []
                    for k in range(A_GROUPS):
                        c = slice((i % 4) * P, (i % 4 + 1) * P)
                        piece = 2 * k + i // 4
                        pairs.append((w_hi[:, slot, piece, c], w_lo[:, slot, piece, c], y_hi[:, k], y_lo[:, k]))

                    def ready(k):
                        if j == 0:
                            pe.wait_ge(s_wlo.sem, s_wlo.at(layer, NQ * g + k + 1))
                            pe.wait_ge(done.sem, done.at(layer, k + 1))
                else:
                    tok = slice(j * P, (j + 1) * P)
                    if name in TOKEN_MAJOR:
                        pairs = [(h_hi[:, k, tok], h_lo[:, k, tok], w_hi[:, slot, k], w_lo[:, slot, k])
                                 for k in range(KD)]
                    else:
                        pairs = [(w_hi[:, slot, k, tok], w_lo[:, slot, k, tok], h_hi[:, k], h_lo[:, k])
                                 for k in range(KD)]
                    if name == "iq":
                        pe.wait_ge(s_hlo.sem, s_hlo.at(layer, 2 * (j + 1)))

                    def ready(k):
                        if j == 0 and k % 2 == 0:
                            pe.wait_ge(s_wlo.sem, s_wlo.at(layer, NQ * g + k // 2 + 1))
                        if name == "out" and n == JOB_OUT[0]:
                            pe.wait_ge(s_mlo.sem, s_mlo.at(layer, k + 1))
                last = three_pass(dst[:], pairs, ready)
                if name == "iq":
                    if j == 0:
                        pe.wait_ge(s_slo.sem, s_slo.at(layer, 1))
                    pe.wait_ge(s_small.sem, s_small.at(layer, j))
                    tok = slice(j * P, (j + 1) * P)
                    last = three_pass(bank[7][:, j * SMALL:(j + 1) * SMALL],
                                      [(h_hi[:, k, tok], h_lo[:, k, tok], s_hi[:, k], s_lo[:, k]) for k in range(KD)])
                last.then_inc(s_job.sem, 1)

            with pe.Fori(0, DEPTH) as layer:
                transpose_x(layer, 0)
                transpose_x(layer, 1)
                for g in range(len(GROUPS)):
                    for j in range(GROUPS[g][3]):
                        n = FIRST_JOB[g] + j
                        job(layer, g, j)
                        if n + 2 < TILES:
                            transpose_x(layer, n + 2)
                        if n in AFTER_QI:
                            transpose_rotated(layer, AFTER_QI[n])
                        if n in AFTER_K:
                            transpose_rotated(layer, TILES + AFTER_K[n])
                        if n in AFTER_Q:
                            transpose_rotated(layer, 2 * TILES + AFTER_Q[n])
                        for step in AFTER_IDX.get(n, []):
                            index_logits(layer, step)
                        if n == AFTER_WS:
                            transpose_ws(layer)
                        for group in AFTER_MIX.get(n, []):
                            mix(layer, group)
                        if n in AFTER_ATT:
                            attend(layer, AFTER_ATT[n])

        @block.scalar
        def _(act):
            seed(act, s_whi, s_shi, s_xstd, s_hhi, s_small, s_stage, s_rotc, s_relu, s_vb, s_va, s_u, s_wsc,
                 s_lnstd, s_tanh, s_yahi, s_ga, s_gb, s_mhi, s_exp, s_ptc, s_ybhi, *s_free)

            def rounded(layer, g, qt):
                n = g * NQ + qt
                act.wait_ge(s_wraw[n % RAW].sem, s_wraw[n % RAW].at(layer, 16 * (n // RAW + 1)))
                act.wait_ge(s_job.sem, slot_free(layer, g))
                nc.scalar.activation(w_hi[:, w_slot(g), 2 * qt:2 * qt + 2], w_raw[:, n % RAW], ACT.Copy) \
                    .then_inc(s_whi.sem, 1)

            def root(layer, dst, src, scale=1.0):
                return nc.scalar.activation(dst, src, ACT.Sqrt, bias=eps[:], scale=scale)

            def head_std(layer, n, src):
                c = HEADS * n
                for h in range(HEADS):
                    act_.mark(nc.scalar.activation(bank[7][:, h * DH:(h + 1) * DH], src[:, h * DH:(h + 1) * DH], ACT.Square,
                                                   scale=DH ** -0.5, accum_out=ms[:, c + h:c + h + 1]))
                act_.join(act)
                act_.mark(root(layer, std[:, c:c + HEADS], ms[:, c:c + HEADS]))

            def evacuate(layer, n):
                src, free = bank[n % GBANKS], s_free[n % GBANKS]
                act.wait_ge(s_job.sem, s_job.at(layer, n + 1))
                if n in JOB_IQ:
                    t = n - JOB_IQ[0]
                    act.wait_ge(s_rot.sem, s_rot.at(layer, t - 1))
                    if t == 0:
                        act.wait_ge(s_zused.sem, s_zused.at(layer, 0))
                    nc.scalar.activation(stage[:, t % 2, 0:IH * ID], src[:], ACT.Copy).then_inc(free.sem, 1)
                    act_.mark(nc.scalar.activation(stage[:, t % 2, IH * ID:IH * ID + SMALL],
                                                   bank[7][:, t * SMALL:(t + 1) * SMALL], ACT.Copy))
                    act_.join(act)
                    act.sem_inc(s_small.sem, 1)
                    act.sem_inc(s_stage.sem, 1)
                elif n in JOB_K or n in JOB_Q:
                    t = n - JOB_K[0]
                    act.wait_ge(s_rot.sem, s_rot.at(layer, TILES + t - 1))
                    head_std(layer, t, src)
                    act_.mark(nc.scalar.activation(stage[:, (TILES + t) % 2, 0:HEADS * DH], src[:], ACT.Copy))
                    act_.join(act)
                    act.sem_inc(free.sem, 1)
                    act.sem_inc(s_stage.sem, 1)
                elif n in JOB_VB:
                    t = n - JOB_VB[0]
                    act_.mark(nc.scalar.activation(v_b[:, t], src[:], ACT.Copy))
                    act_.join(act)
                    act.sem_inc(free.sem, 1)
                    act.sem_inc(s_vb.sem, 1)
                elif n in JOB_VA or n in JOB_U:
                    dst, done, t = (v_a, s_va, n - JOB_VA[0]) if n in JOB_VA else (u_a, s_u, n - JOB_U[0])
                    act_.mark(nc.scalar.activation(dst[:, t], src[:], ACT.Gelu_apprx_tanh))
                    act_.join(act)
                    act.sem_inc(free.sem, 1)
                    act.sem_inc(done.sem, 1)
                elif n in JOB_ZB or n in JOB_ZA:
                    t = n - JOB_ZB[0]
                    if n == JOB_ZB[0]:
                        act.wait_ge(s_lnv.sem, s_lnv.at(layer, 1))
                        root(layer, ln_std[:], mv[:, :, 1]).then_inc(s_lnstd.sem, 1)
                    act.wait_ge(s_zused.sem, s_zused.at(layer, t - 1))
                    if t == 0:
                        act.wait_ge(s_rot.sem, s_rot.at(layer, 3 * TILES))
                    nc.scalar.activation(t_half[:, t % 2], src[:], ACT.Tanh, scale=0.5).then_inc(s_tanh.sem, 1)
                elif n in JOB_GA or n in JOB_GB:
                    dst, done, d, c = (g_a, s_ga, n - JOB_GA[0], 0) if n in JOB_GA else (g_b, s_gb, n - JOB_GB[0], KD)
                    if n == JOB_GA[0]:
                        act.wait_ge(s_mix.sem, s_mix.at(layer, A_GROUPS))
                        act.wait_ge(s_ghalf.sem, s_ghalf.at(layer, 1))
                    if n == JOB_GA[4]:
                        act.wait_ge(s_yalo.sem, s_yalo.at(layer, A_GROUPS))
                    if n == JOB_GB[0]:
                        act.wait_ge(s_job.sem, s_job.at(layer, JOB_OA[-1] + 1))
                    act_.mark(nc.scalar.activation(dst[:, d], src[:], ACT.Tanh, scale=0.5,
                                                   bias=gate_half[:, c + d:c + d + 1]))
                    act_.join(act)
                    act.sem_inc(free.sem, 1)
                    act.sem_inc(done.sem, 1)

            def beside(layer, n):
                for after, base in ((AFTER_QI, 0), (AFTER_K, TILES), (AFTER_Q, 2 * TILES)):
                    if n in after:
                        t = after[n]
                        act.wait_ge(s_rott.sem, s_rott.at(layer, base + t + 1))
                        four = bank[5][:].rearrange("p (c q) -> p c q", c=4)
                        if base == 0:
                            if t == 0:
                                act.wait_ge(s_out.sem, s_out.at(layer, 0))
                                act.wait_ge(s_xt.sem, s_xt.at(layer, 2 * TILES))
                            if t:
                                act_.mark(nc.scalar.activation(qi_t[:, :, (t - 1) * P:t * P], four, ACT.Copy))
                            act_.mark(nc.scalar.activation(ki_t[:, t * P:(t + 1) * P], bank[6][:, 0:P], ACT.Copy))
                        else:
                            dst = k_t if base == TILES else q_t
                            act_.mark(nc.scalar.activation(dst[:, :, t * P:(t + 1) * P], four, ACT.Copy))
                        act_.join(act)
                        act.sem_inc(s_rotc.sem, 1)
                for i in AFTER_IDX.get(n, []):
                    b, h = IDX_STEPS[i]
                    w = P * (b + 1)
                    act.wait_ge(s_idxp.sem, s_idxp.at(layer, i + 1))
                    if i >= 2:
                        act.wait_ge(s_idx.sem, s_idx.at(layer, i - 1))
                    nc.scalar.activation(probs[:, i % 2, 0:w], bank[3 + i % 2][:, 0:w], ACT.Relu).then_inc(s_relu.sem, 1)
                if n == AFTER_WS:
                    act.wait_ge(s_wst.sem, s_wst.at(layer, 1))
                    four = bank[5][:].rearrange("p (c q) -> p c q", c=A_GROUPS)
                    act_.mark(nc.scalar.activation(ws_t[0:CHUNK], four[0:CHUNK], ACT.Copy))
                    act_.mark(nc.scalar.activation(ws_t[CHUNK:P, :, CHUNK:P], four[CHUNK:P, :, CHUNK:P], ACT.Copy))
                    act_.join(act)
                    act.sem_inc(s_wsc.sem, 1)
                if n - 1 in JOB_ZA:
                    c = n - 1 - JOB_ZA[0]
                    act.wait_ge(s_ya.sem, s_ya.at(layer, c + 1))
                    nc.scalar.activation(ya_hi[:, c], u_a[:, c], ACT.Copy).then_inc(s_yahi.sem, 1)
                if n in AFTER_ATT:
                    i = AFTER_ATT[n]
                    if i >= 1 and i <= len(ATT_STEPS):
                        b = ATT_STEPS[i - 1][1]
                        w = P * (b + 1)
                        act.wait_ge(s_pt.sem, s_pt.at(layer, i))
                        if i >= 2:
                            act.wait_ge(s_pv.sem, s_pv.at(layer, i - 1))
                        nc.scalar.activation(probs_t[:, 0:w], bank[5][:, 0:w], ACT.Copy).then_inc(s_ptc.sem, 1)
                    if i < len(ATT_STEPS):
                        w = P * (ATT_STEPS[i][1] + 1)
                        act.wait_ge(s_max.sem, s_max.at(layer, i + 1))
                        act_.mark(nc.scalar.activation(probs[:, i % 2, 0:w], probs[:, i % 2, 0:w], ACT.Exp,
                                                       bias=neg_max[:, i:i + 1], scale=ATT_SCALE,
                                                       accum_out=row_sum[:, i:i + 1]))
                        act_.join(act)
                        act.sem_inc(s_exp.sem, 1)
                    if i >= 2 and ATT_STEPS[i - 2][1] == TILES - 1:
                        h = ATT_STEPS[i - 2][0]
                        act.wait_ge(s_yb.sem, s_yb.at(layer, h + 1))
                        nc.scalar.activation(yb_hi[:, h], z_b[:, h], ACT.Copy).then_inc(s_ybhi.sem, 1)
                if n in JOB_OB:
                    d = n - JOB_OB[0]
                    act.wait_ge(s_sum.sem, s_sum.at(layer, d + 1))
                    if d == 0:
                        act.wait_ge(s_job.sem, s_job.at(layer, JOB_GB[-1] + 1))
                    nc.scalar.activation(h_hi[:, d], g_b[:, d], ACT.Copy, scale=0.5).then_inc(s_mhi.sem, 1)

            def x_std(layer, t):
                c = 2 * TILES * HEADS + t
                act.wait_ge(s_res.sem, s_res.at(layer, t + 1 - TILES))
                if t >= 2:
                    act.wait_ge(s_xt.sem, s_xt.at(layer, 2 * (t - 1)))
                act_.link(act, nc.scalar.activation(xn[:, t % 2], x_sb[:, t], ACT.Square, scale=D ** -0.5,
                                                    accum_out=ms[:, c:c + 1]))
                root(layer, std[:, c:c + 1], ms[:, c:c + 1]).then_inc(s_xstd.sem, 1)

            def h_rounded(layer, t):
                act.wait_ge(s_job.sem, s_job.at(layer, JOB_OUT[TILES + t] + 1 - NJOBS))
                for half in range(2):
                    act.wait_ge(s_xt.sem, s_xt.at(layer, 2 * t + half + 1))
                    nc.scalar.activation(h_hi[:, 4 * half:4 * half + 4, t * P:(t + 1) * P],
                                         bank[3 + 2 * (t % 2) + half][:].rearrange("p (c q) -> p c q", c=4),
                                         ACT.Copy).then_inc(s_hhi.sem, 1)

            act.wait_ge(s_init, 1)
            act.wait_ge(s_x0, 16 * TILES)
            with act.Fori(0, DEPTH) as layer:
                for t in range(2):
                    x_std(layer, t)
                    rounded(layer, 0, 2 * t)
                    rounded(layer, 0, 2 * t + 1)
                    h_rounded(layer, t)
                act.wait_ge(s_par.sem, s_par.at(layer, 16 * 9))
                nc.scalar.activation(s_hi[:], s_raw[:], ACT.Copy).then_inc(s_shi.sem, 1)
                for n in range(NJOBS):
                    if n + 2 < TILES:
                        x_std(layer, n + 2)
                    if quarter_in(n):
                        rounded(layer, *quarter_in(n))
                    evacuate(layer, n)
                    if n + 2 < TILES:
                        h_rounded(layer, n + 2)
                    beside(layer, n)
                pause(act)
                act_.end_layer(act)

        @block.vector
        def _(dve):
            seed(dve, s_wlo, s_slo, s_ghalf, s_xn, s_hlo, s_rinv, s_rot, s_idx, s_wsz, s_lnv, s_ln, s_um, s_zused,
                 s_ya, s_yalo, s_ma, s_sum, s_mlo, s_max, s_prob, s_yb, s_yblo, s_res)
            vec.mark(nc.vector.memset(diag[:], 0.0))
            vec.join(dve)
            vec.mark(nc.vector.memset(diag[0:CHUNK, CHUNK:P], FILL))
            vec.mark(nc.vector.memset(eps[:], EPS))
            vec.join(dve)
            dve.sem_inc(s_init, 1)
            vec.end_layer(dve)

            def remainder(layer, g, qt):
                n = g * NQ + qt
                dve.wait_ge(s_whi.sem, s_whi.at(layer, n + 1))
                nc.vector.tensor_tensor(w_lo[:, w_slot(g), 2 * qt:2 * qt + 2], w_raw[:, n % RAW],
                                        w_hi[:, w_slot(g), 2 * qt:2 * qt + 2].bitcast(F32), ALU.subtract) \
                    .then_inc(s_wlo.sem, 1)

            def rotate(tile, heads, dim, cos, sin):
                w, half = heads * dim, dim // 2
                src = tile[:, 0:w].rearrange("p (h d) -> p h d", h=heads)
                a = rope_a[:, 0:w].rearrange("p (h d) -> p h d", h=heads)
                b = rope_b[:, 0:w].rearrange("p (h d) -> p h d", h=heads)
                vec.mark(nc.vector.tensor_tensor(a, src, cos.unsqueeze(1).to_broadcast([P, heads, dim]), ALU.mult))
                for lo, hi in ((slice(0, half), slice(half, dim)), (slice(half, dim), slice(0, half))):
                    vec.mark(nc.vector.tensor_tensor(b[:, :, lo], src[:, :, hi],
                                                     sin[:, lo].unsqueeze(1).to_broadcast([P, heads, half]), ALU.mult))
                vec.join(dve)
                return nc.vector.tensor_tensor(rot[:, 0:w], rope_a[:, 0:w], rope_b[:, 0:w], ALU.add)

            def rotated(layer, n):
                dve.wait_ge(s_rott.sem, s_rott.at(layer, n))
                if n < TILES:
                    dve.wait_ge(s_stage.sem, s_stage.at(layer, n + 1))
                    tile = stage[:, n % 2]
                    vec.mark(nc.vector.tensor_scalar(head_w[:, n], tile[:, ROT_I:ROT_I + IH], IDX_SCALE, None, ALU.mult))
                    vec.mark(rotate(tile, IH + 1, ID, ci[:, n], si[:, n]))
                    vec.join(dve)
                    nc.vector.tensor_copy(rot[:, ROT_I:ROT_I + ID], rot[:, IH * ID:ROT_I]).then_inc(s_rot.sem, 1)
                else:
                    m = n - TILES
                    dve.wait_ge(s_xg.sem, s_xg.at(layer, m + 1))
                    rotate(stage[:, n % 2], HEADS, DH, cq[:, m % TILES], sq[:, m % TILES]).then_inc(s_rot.sem, 1)

            def index_add(layer, i):
                b, h = IDX_STEPS[i]
                cols, w = block_cols(b), P * (b + 1)
                weight = head_w[:, b, h:h + 1]
                dve.wait_ge(s_relu.sem, s_relu.at(layer, i + 1))
                if h == 0:
                    op = nc.vector.tensor_scalar(score[:, cols], probs[:, i % 2, 0:w], weight, None, ALU.mult)
                else:
                    op = nc.vector.scalar_tensor_tensor(score[:, cols], probs[:, i % 2, 0:w], weight, score[:, cols],
                                                        ALU.mult, ALU.add)
                op.then_inc(s_idx.sem, 1)
                dve.wait_ge(s_idx.sem, s_idx.at(layer, i + 1))
                if h == IH - 1:
                    last = score[:, cols.stop - P:cols.stop]
                    vec.link(dve, nc.vector.tensor_tensor(last, last, diag[:], ALU.add))

            def topk_round(b, r):
                s = score[:, block_cols(b)]
                vec.link(dve, nc.vector.max(top8[:], s))
                vec.link(dve, nc.vector.match_replace(s, top8[:], s, TAKEN))
                if r == ROUNDS - 1:
                    vec.link(dve, nc.vector.tensor_scalar(s, s, TAKEN, FILL, ALU.not_equal, ALU.mult))

            def attention_scale(layer, i):
                w = P * (ATT_STEPS[i][1] + 1)
                dve.wait_ge(s_exp.sem, s_exp.at(layer, i + 1))
                vec.link(dve, nc.vector.reciprocal(row_inv[:, i:i + 1], row_sum[:, i:i + 1]))
                nc.vector.tensor_scalar(probs[:, i % 2, 0:w], probs[:, i % 2, 0:w], row_inv[:, i:i + 1], None,
                                        ALU.mult).then_inc(s_prob.sem, 1)

            def attention_max(layer, i):
                b = ATT_STEPS[i][1]
                w = P * (b + 1)
                mask = score[:, block_cols(b)] if b else diag[:]
                dve.wait_ge(s_qk.sem, s_qk.at(layer, i + 1))
                if i >= 2:
                    dve.wait_ge(s_pt.sem, s_pt.at(layer, i - 1))
                pause(dve)
                vec.link(dve, nc.vector.tensor_tensor_reduce(
                    out=probs[:, i % 2, 0:w], in0=bank[3 + i % 2][:, 0:w], in1=mask, scale=1.0, scalar=2 * FILL,
                    op0=ALU.add, op1=ALU.max, accum_out=row_max[:, i:i + 1]))
                nc.vector.tensor_scalar(neg_max[:, i:i + 1], row_max[:, i:i + 1], -ATT_SCALE, None,
                                        ALU.mult).then_inc(s_max.sem, 1)

            def evacuate(layer, n):
                src, free = bank[n % GBANKS], s_free[n % GBANKS]
                if n in JOB_K or n in JOB_Q:
                    m = n - JOB_K[0]
                    c = HEADS * m
                    dve.wait_ge(s_stage.sem, s_stage.at(layer, TILES + m + 1))
                    nc.vector.reciprocal(rstd[:, c:c + HEADS], std[:, c:c + HEADS]).then_inc(s_rinv.sem, 1)
                elif n in JOB_VA:
                    t = n - JOB_VA[0]
                    dve.wait_ge(s_va.sem, s_va.at(layer, t + 1))
                    vec.link(dve, nc.vector.bn_stats(bn[:, t], v_a[:, t]))
                    op = nc.vector.bn_aggr(mv[:, t], bn[:, t])
                    if t < TILES - 1:
                        vec.mark(op)
                    else:
                        vec.link(dve, op)
                        dve.sem_inc(s_lnv.sem, 1)
                elif n in JOB_ZB:
                    c = n - JOB_ZB[0]
                    dve.wait_ge(s_tanh.sem, s_tanh.at(layer, c + 1))
                    if c == 0:
                        dve.wait_ge(s_idxp.sem, s_idxp.at(layer, len(IDX_STEPS)))
                    vec.link(dve, nc.vector.scalar_tensor_tensor(z_b[:, c], t_half[:, c % 2], 1.0, src[:],
                                                                 ALU.add, ALU.mult))
                    dve.sem_inc(free.sem, 1)
                    dve.sem_inc(s_zused.sem, 1)
                elif n in JOB_ZA:
                    c = n - JOB_ZA[0]
                    dve.wait_ge(s_tanh.sem, s_tanh.at(layer, 4 + c + 1))
                    vec.link(dve, nc.vector.scalar_tensor_tensor(silu_z[:], t_half[:, c % 2], 1.0, src[:],
                                                                 ALU.add, ALU.mult))
                    dve.sem_inc(free.sem, 1)
                    dve.sem_inc(s_zused.sem, 1)
                    vec.link(dve, nc.vector.scalar_tensor_tensor(u_a[:, c], silu_z[:], SILU_HALF, u_a[:, c],
                                                                 ALU.mult, ALU.mult))
                    dve.sem_inc(s_ya.sem, 1)
                elif n in JOB_OA:
                    d = n - JOB_OA[0]
                    dve.wait_ge(s_job.sem, s_job.at(layer, n + 1))
                    dve.wait_ge(s_ga.sem, s_ga.at(layer, d + 1))
                    vec.link(dve, nc.vector.scalar_tensor_tensor(g_a[:, d], g_a[:, d], 1.0, src[:], ALU.add, ALU.mult))
                    dve.sem_inc(free.sem, 1)
                    dve.sem_inc(s_ma.sem, 1)
                elif n in JOB_OB:
                    d = n - JOB_OB[0]
                    dve.wait_ge(s_job.sem, s_job.at(layer, n + 1))
                    dve.wait_ge(s_gb.sem, s_gb.at(layer, d + 1))
                    vec.link(dve, nc.vector.scalar_tensor_tensor(g_b[:, d], g_b[:, d], 1.0, src[:], ALU.add, ALU.mult))
                    dve.sem_inc(free.sem, 1)
                    nc.vector.tensor_tensor(g_b[:, d], g_b[:, d], g_a[:, d], ALU.add).then_inc(s_sum.sem, 1)
                elif n in JOB_OUT:
                    i = n - JOB_OUT[0]
                    t, half = i % TILES, i // TILES
                    dve.wait_ge(s_job.sem, s_job.at(layer, n + 1))
                    if i == 0:
                        dve.wait_ge(s_xback.sem, s_xback.at(layer, 16))
                    part = x_sb[:, t, half * W512:(half + 1) * W512]
                    vec.link(dve, nc.vector.tensor_tensor(part, part, src[:], ALU.add))
                    dve.sem_inc(free.sem, 1)
                    dve.sem_inc(s_res.sem, 1)

            def ln_apply(layer, t):
                tile = v_a[:, t]
                vec.link(dve, nc.vector.tensor_scalar(tile, tile, mv[:, t, 0:1], ln_rstd[:, t:t + 1],
                                                      ALU.subtract, ALU.mult))
                vec.link(dve, nc.vector.tensor_tensor(tile, tile, lng_bc[:], ALU.mult))
                nc.vector.tensor_tensor(tile, tile, lnb_bc[:], ALU.add).then_inc(s_ln.sem, 1)

            def beside(layer, n):
                if n in JOB_IQ:
                    rotated(layer, n - JOB_IQ[0])
                if n in JOB_K or n in JOB_Q:
                    rotated(layer, TILES + n - JOB_K[0])
                for i in AFTER_IDX.get(n, []):
                    index_add(layer, i)
                if n == JOB_VB[0]:
                    nc.vector.memset(ws_t[CHUNK:P, :, 0:CHUNK], 0.0).then_inc(s_wsz.sem, 1)
                    dve.wait_ge(s_par.sem, s_par.at(layer, 16 * 9))
                    nc.vector.tensor_scalar(gate_half[:], gate_raw[:], 0.5, None, ALU.mult).then_inc(s_ghalf.sem, 1)
                if n == JOB_ZB[0]:
                    dve.wait_ge(s_lnstd.sem, s_lnstd.at(layer, 1))
                    vec.link(dve, nc.vector.reciprocal(ln_rstd[:], ln_std[:]))
                if n in JOB_ZB[0:2]:
                    for t in range(2 * (n - JOB_ZB[0]), 2 * (n - JOB_ZB[0]) + 2):
                        ln_apply(layer, t)
                for g in AFTER_MIX.get(n, []):
                    dve.wait_ge(s_mix.sem, s_mix.at(layer, g + 1))
                    dve.wait_ge(s_u.sem, s_u.at(layer, TILES))
                    m = bank[3 + g][:].rearrange("p (n i) -> p n i", n=TILES)
                    biased = um[:, 0:SEQ].rearrange("p (n i) -> p n i", n=TILES)
                    vec.link(dve, nc.vector.tensor_tensor(biased, m, bs_bc[:, g].unsqueeze(1).to_broadcast([P, TILES, P]),
                                                          ALU.add))
                    vec.link(dve, nc.vector.tensor_tensor(u_a[:, g], um[:, 0:SEQ], u_a[:, g], ALU.mult))
                    dve.sem_inc(s_um.sem, 1)
                if n - 1 in JOB_ZA:
                    c = n - 1 - JOB_ZA[0]
                    dve.wait_ge(s_yahi.sem, s_yahi.at(layer, c + 1))
                    nc.vector.tensor_tensor(ya_lo[:, c], u_a[:, c], ya_hi[:, c].bitcast(F32), ALU.subtract) \
                        .then_inc(s_yalo.sem, 1)
                if n in AFTER_ATT:
                    i = AFTER_ATT[n]
                    if i < len(ATT_STEPS):
                        attention_max(layer, i)
                    if i >= 2 and ATT_STEPS[i - 2][1] == TILES - 1:
                        h = ATT_STEPS[i - 2][0]
                        dve.wait_ge(s_pv.sem, s_pv.at(layer, i - 1))
                        vec.link(dve, nc.vector.scalar_tensor_tensor(z_b[:, h], z_b[:, h], SILU_HALF, bank[7][:],
                                                                     ALU.mult, ALU.mult))
                        dve.sem_inc(s_yb.sem, 1)
                        dve.wait_ge(s_ybhi.sem, s_ybhi.at(layer, h + 1))
                        nc.vector.tensor_tensor(yb_lo[:, h], z_b[:, h], yb_hi[:, h].bitcast(F32), ALU.subtract) \
                            .then_inc(s_yblo.sem, 1)
                    if i < len(ATT_STEPS):
                        attention_scale(layer, i)
                if n in JOB_OB:
                    d = n - JOB_OB[0]
                    dve.wait_ge(s_mhi.sem, s_mhi.at(layer, d + 1))
                    nc.vector.scalar_tensor_tensor(h_lo[:, d], g_b[:, d], 0.5, h_hi[:, d].bitcast(F32),
                                                   ALU.mult, ALU.subtract).then_inc(s_mlo.sem, 1)

            def x_normalised(layer, t):
                c = 2 * TILES * HEADS + t
                dve.wait_ge(s_xstd.sem, s_xstd.at(layer, t + 1))
                vec.link(dve, nc.vector.reciprocal(rstd[:, c:c + 1], std[:, c:c + 1]))
                nc.vector.scalar_tensor_tensor(xn[:, t % 2], x_sb[:, t], rstd[:, c:c + 1], norm_bc[:],
                                               ALU.mult, ALU.mult).then_inc(s_xn.sem, 1)

            def h_remainder(layer, t):
                for half in range(2):
                    dve.wait_ge(s_hhi.sem, s_hhi.at(layer, 2 * t + half + 1))
                    dst = slice(4 * half, 4 * half + 4), slice(t * P, (t + 1) * P)
                    nc.vector.tensor_tensor(h_lo[:, dst[0], dst[1]],
                                            bank[3 + 2 * (t % 2) + half][:].rearrange("p (c q) -> p c q", c=4),
                                            h_hi[:, dst[0], dst[1]].bitcast(F32), ALU.subtract) \
                        .then_inc(s_hlo.sem, 1)

            dve.wait_ge(s_const, 16 * 5)
            with dve.Fori(0, DEPTH) as layer:
                dve.wait_ge(s_par.sem, s_par.at(layer, 16 * 9))
                for t in range(2):
                    x_normalised(layer, t)
                    remainder(layer, 0, 2 * t)
                    remainder(layer, 0, 2 * t + 1)
                    h_remainder(layer, t)
                dve.wait_ge(s_shi.sem, s_shi.at(layer, 1))
                nc.vector.tensor_tensor(s_lo[:], s_raw[:], s_hi[:].bitcast(F32), ALU.subtract).then_inc(s_slo.sem, 1)
                done = {b: 0 for b in range(1, TILES)}
                for n in range(NJOBS):
                    if n + 2 < TILES:
                        x_normalised(layer, n + 2)
                    if quarter_in(n):
                        remainder(layer, *quarter_in(n))
                    if n + 2 < TILES:
                        h_remainder(layer, n + 2)
                    evacuate(layer, n)
                    beside(layer, n)
                    for s, b, count in TOPK_SLOTS:
                        if s == n:
                            pause(dve)
                        for _ in range(min(count, ROUNDS - done[b]) if s == n else 0):
                            topk_round(b, done[b])
                            done[b] += 1
                assert all(v == ROUNDS for v in done.values())
                pause(dve)
                vec.end_layer(dve)


def rope_tables(dim):
    inv = (ROPE_THETA ** (-np.arange(0, dim, 2, dtype=np.float64) / dim)).astype(np.float32)
    ang = np.arange(SEQ, dtype=np.float32)[:, None] * inv[None, :]
    cos, sin = np.cos(ang), np.sin(ang)
    lay = lambda a: np.ascontiguousarray(a.astype(np.float32).reshape(TILES, P, dim).transpose(1, 0, 2))
    return lay(np.concatenate([cos, cos], 1)), lay(np.concatenate([-sin, sin], 1))


def kernel(x, norm_g, w_in, gate_b, a_ln_g, a_ln_b, a_ws, a_bs, q_norm_g, k_norm_g, w_oa, w_ob, w_out):
    import concourse.bacc as bacc
    from concourse.bass_utils import run_bass_kernel_spmd

    cos_qk, sin_qk = rope_tables(DH)
    cos_i, sin_i = rope_tables(ID)
    gate = np.asarray(gate_b).reshape(DEPTH, 2, KD, P).transpose(0, 3, 1, 2).reshape(DEPTH, P, 2 * KD)
    arrays = dict(x=np.asarray(x).reshape(SEQ, D), norm_g=norm_g, w_in=w_in, gate_b=gate, a_ln_g=a_ln_g,
                  a_ln_b=a_ln_b, a_ws=a_ws, a_bs=np.asarray(a_bs).reshape(DEPTH, A_GROUPS * P), q_norm_g=q_norm_g,
                  k_norm_g=k_norm_g, w_oa=w_oa, w_ob=w_ob, w_out=w_out, ident=np.eye(P, dtype=np.float32),
                  cos_qk=cos_qk, sin_qk=sin_qk, cos_i=cos_i, sin_i=sin_i)
    arrays = {k: np.ascontiguousarray(v) for k, v in arrays.items()}
    nc = bacc.Bacc("TRN2", target_bir_lowering=False, num_devices=1)
    aps = {k: nc.dram_tensor(f"in_{k}", v.shape, F32, kind="ExternalInput").ap() for k, v in arrays.items()}
    out = nc.dram_tensor("out", (SEQ, D), F32, kind="ExternalOutput").ap()
    trunk(nc, **aps, out=out)
    r = run_bass_kernel_spmd(nc, [{f"in_{k}": v for k, v in arrays.items()}], core_ids=[0])
    return r.results[0]["out"].reshape(1, SEQ, D)
```

```python
from contextlib import ExitStack

import concourse.bass as bass
import numpy as np
from concourse import mybir
from concourse.alu_op_type import AluOpType as ALU

F32 = mybir.dt.float32
F32R = mybir.dt.float32r
ACT = mybir.ActivationFunctionType
AX = mybir.AxisListType

P = 128
DEPTH, SEQ, D = 2, 512, 1024
CHUNK = 64
EPS = 1e-6
ROPE_THETA = 10000.0
A_WIDTH, A_GROUPS = 512, 4
HEADS, DH = 4, 128
IH, ID = 8, 64
TOPK = min(256, SEQ // 4)
SPLITS = dict(u=A_WIDTH, va=A_WIDTH, za=A_WIDTH, q=HEADS * DH, k=HEADS * DH, vb=HEADS * DH, zb=HEADS * DH,
              iq=IH * ID, ik=ID, iw=IH, ga=D, gb=D)
COL = dict(zip(SPLITS, np.cumsum([0] + list(SPLITS.values())[:-1]).tolist()))
IN_WIDTH = sum(SPLITS.values())

TILES = SEQ // P
KD = D // P
W512 = 512
SMALL = ID + IH
ROT_I = (IH + 1) * ID
ATT_SCALE = DH ** -0.5
IDX_SCALE = ID ** -0.5 * IH ** -0.5
FILL = -(2.0 ** 126)
TAKEN = -(2.0 ** 127)
SILU_HALF = 0.5

GROUPS = [
    ("iq", "w_in", COL["iq"], 4), ("k", "w_in", COL["k"], 4), ("q", "w_in", COL["q"], 4),
    ("vb", "w_in", COL["vb"], 4), ("va", "w_in", COL["va"], 4), ("u", "w_in", COL["u"], 4),
    ("zb", "w_in", COL["zb"], 4), ("za", "w_in", COL["za"], 4),
    ("ga", "w_in", COL["ga"], 4), ("ga", "w_in", COL["ga"] + W512, 4),
    ("oa", "w_oa", 0, 8),
    ("gb", "w_in", COL["gb"], 4), ("gb", "w_in", COL["gb"] + W512, 4),
    ("ob", "w_ob", 0, 8),
    ("out", "w_out", 0, 4), ("out", "w_out", W512, 4),
]
N_PARAMS = 7
TOKEN_MAJOR = {"iq", "k", "q", "vb", "va", "out"}
FIRST_JOB = np.cumsum([0] + [g[3] for g in GROUPS]).tolist()
NJOBS = FIRST_JOB[-1]
NQ = 4
RAW = 4
GBANKS = 3
assert NJOBS % GBANKS == 0 and (len(GROUPS) * NQ) % RAW == 0


def jobs_of(name):
    return [FIRST_JOB[g] + j for g in range(len(GROUPS)) if GROUPS[g][0] == name for j in range(GROUPS[g][3])]


JOB_IQ, JOB_K, JOB_Q, JOB_VB, JOB_VA, JOB_U, JOB_ZB, JOB_ZA, JOB_GA, JOB_OA, JOB_GB, JOB_OB, JOB_OUT = (
    jobs_of(n) for n in ("iq", "k", "q", "vb", "va", "u", "zb", "za", "ga", "oa", "gb", "ob", "out"))

AFTER_QI = {JOB_IQ[t] + 2: t for t in range(TILES)}
AFTER_K = {JOB_K[t] + 2: t for t in range(TILES)}
AFTER_Q = {JOB_Q[t] + 2: t for t in range(TILES)}
IDX_STEPS = [(b, h) for b in range(1, TILES) for h in range(IH)]
AFTER_IDX = {6 + n // 2: [n - n % 2, n - n % 2 + 1] for n in range(len(IDX_STEPS))}
AFTER_WS = JOB_VA[2]
LN_TILES = {JOB_ZB[0]: [0, 1], JOB_ZB[1]: [2], JOB_ZB[2]: [3]}
AFTER_MIX = {JOB_ZB[3]: [0, 1], JOB_ZA[0]: [2, 3]}
ATT_STEPS = [(h, b) for b in range(TILES) for h in range(HEADS)]
_slots = list(range(JOB_ZA[2], JOB_GA[-1] + 1)) + JOB_OA[1::2] + JOB_GB
AFTER_ATT = {_slots[i]: i for i in range(len(ATT_STEPS) + 2)}
SPLIT_YB = {JOB_GB[4 + h]: h for h in range(HEADS)}
assert min(SPLIT_YB) > max(AFTER_ATT)
ROUNDS = TOPK // 8
TOPK_SLOTS = ([(s, 1, 2) for s in range(12, 20)] + [(s, 2, 2) for s in range(20, 24)]
              + [(s, 2, 1) for s in range(24, 32)] + [(s, 3, 2) for s in range(32, 40)])


class Signal:

    def __init__(self, ctx, nc, name, per_layer, seeded=True):
        self.sem, self.per = ctx.enter_context(nc.semaphore(name)), per_layer
        self.seeded = seeded

    def at(self, layer, n):
        return layer * self.per + (self.per if self.seeded else 0) + n


class Steps:

    def __init__(self, ctx, nc, name):
        self.sem, self.n, self.waited = ctx.enter_context(nc.semaphore(name)), 0, 0

    def link(self, engine, instruction):
        self.mark(instruction)
        self.join(engine)

    def mark(self, instruction):
        self.n += 1
        instruction.then_inc(self.sem, 1)

    def join(self, engine):
        if self.n > self.waited:
            engine.wait_ge(self.sem, self.n)
            self.waited = self.n

    def end_layer(self, engine):
        self.join(engine)
        engine.sem_clear(self.sem)
        self.n = self.waited = 0


def trunk(nc, x, norm_g, w_in, gate_b, a_ln_g, a_ln_b, a_ws, a_bs, q_norm_g, k_norm_g, w_oa, w_ob, w_out,
          ident, cos_qk, sin_qk, cos_i, sin_i, out):
    ctx = ExitStack()
    with ctx:
        def sb(name, shape, dt=F32, keep=ctx):
            return keep.enter_context(nc.sbuf_tensor(name, shape, dt))

        w_hi = sb("w_hi", [P, 2, KD, W512], F32R)
        w_lo = sb("w_lo", [P, 2, KD, W512], F32R)
        w_raw = sb("w_raw", [P, RAW, 2, W512])
        h_hi = sb("h_hi", [P, KD, SEQ], F32R)
        h_lo = sb("h_lo", [P, KD, SEQ], F32R)
        with ExitStack() as early:
            xn = sb("xn", [P, 2, D], keep=early)
        with ExitStack() as early:
            k_t = sb("k_t", [P, HEADS, SEQ], keep=early)
            q_t = sb("q_t", [P, HEADS, SEQ], keep=early)
        yb_hi = sb("yb_hi", [P, HEADS, SEQ], F32R)
        yb_lo = sb("yb_lo", [P, HEADS, SEQ], F32R)
        with ExitStack() as early:
            x_sb = sb("x_sb", [P, TILES, D], keep=early)
        v_b = sb("v_b", [P, TILES, HEADS * DH])
        with ExitStack() as early:
            qi_t = sb("qi_t", [P, IH // 2, SEQ - P], keep=early)
            ki_t = sb("ki_t", [P, SEQ], keep=early)
        z_b = sb("z_b", [P, HEADS, SEQ])
        with ExitStack() as early:
            v_a = sb("v_a", [P, TILES, A_WIDTH], keep=early)
            u_a = sb("u_a", [P, A_GROUPS, SEQ], keep=early)
        with ExitStack() as early:
            s_raw = sb("s_raw", [P, KD, SMALL], keep=early)
            s_hi = sb("s_hi", [P, KD, SMALL], F32R, keep=early)
            s_lo = sb("s_lo", [P, KD, SMALL], F32R, keep=early)
        g_a = sb("g_a", [P, KD, SEQ])
        with ExitStack() as early:
            norm_bc = sb("norm_bc", [P, D], keep=early)
            lng_bc = sb("lng_bc", [P, A_WIDTH], keep=early)
            lnb_bc = sb("lnb_bc", [P, A_WIDTH], keep=early)
            bs_bc = sb("bs_bc", [P, A_GROUPS, P], keep=early)
            ws_raw = sb("ws_raw", [P, A_GROUPS, P], keep=early)
            ws_t = sb("ws_t", [P, A_GROUPS, P], keep=early)
            kg_bc = sb("kg_bc", [P, DH], keep=early)
            qg_bc = sb("qg_bc", [P, DH], keep=early)
        with ExitStack() as early:
            ya_hi = sb("ya_hi", [P, A_GROUPS, SEQ], F32R, keep=early)
            ya_lo = sb("ya_lo", [P, A_GROUPS, SEQ], F32R, keep=early)
        g_b = sb("g_b", [P, KD, SEQ])
        with ExitStack() as early:
            stage = sb("stage", [P, 2, ROT_I + IH], keep=early)
            rope_a = sb("rope_a", [P, ROT_I], keep=early)
            rope_b = sb("rope_b", [P, ROT_I], keep=early)
        t_half = sb("t_half", [P, 2, SEQ])
        silu_z = sb("silu_z", [P, SEQ])
        um = sb("um", [P, (2 * (ROT_I + IH) + 2 * ROT_I) - 3 * SEQ])
        rot = sb("rot", [P, ROT_I + ID])
        probs = sb("probs", [P, 2, SEQ])
        probs_t = sb("probs_t", [P, SEQ])
        score = sb("score", [P, sum(P * (b + 1) for b in range(1, TILES))])
        eye = sb("eye", [P, P])
        cq = sb("cq", [P, TILES, DH])
        sq = sb("sq", [P, TILES, DH])
        ci = sb("ci", [P, TILES, ID])
        si = sb("si", [P, TILES, ID])
        diag = sb("diag", [P, P])
        gate_raw = sb("gate_raw", [P, 2 * KD])
        gate_half = sb("gate_half", [P, 2 * KD])
        eps = sb("eps", [P, 1])
        head_w = sb("head_w", [P, TILES, IH])
        top8 = sb("top8", [P, 8])
        ms = sb("ms", [P, 2 * TILES * HEADS + TILES])
        std = sb("std", [P, 2 * TILES * HEADS + TILES])
        rstd = sb("rstd", [P, 2 * TILES * HEADS + TILES])
        bn = sb("bn", [P, TILES, 6])
        mv = sb("mv", [P, TILES, 2])
        ln_std = sb("ln_std", [P, TILES])
        ln_rstd = sb("ln_rstd", [P, TILES])
        row_max = sb("row_max", [P, len(ATT_STEPS)])
        neg_max = sb("neg_max", [P, len(ATT_STEPS)])
        row_sum = sb("row_sum", [P, len(ATT_STEPS)])
        row_inv = sb("row_inv", [P, len(ATT_STEPS)])

        bank = [ctx.enter_context(nc.psum_tensor(f"bank{i}", [P, W512], F32)) for i in range(8)]

        def sig(name, per, seeded=True):
            return Signal(ctx, nc, name, per, seeded)

        s_const = ctx.enter_context(nc.semaphore("constants_in"))
        s_x0 = [ctx.enter_context(nc.semaphore(f"x_in{t}")) for t in range(TILES)]
        s_small_in = sig("small_weights_in", 16, False)
        s_norm = sig("norm_in", 16, False)
        s_par = sig("parameters_in", 16 * N_PARAMS, False)
        s_wraw = [sig(f"weights_raw{i}", 16 * len(GROUPS) * NQ // RAW, False) for i in range(RAW)]
        s_whi = sig("weights_hi", len(GROUPS) * NQ)
        s_wlo = sig("weights_lo", len(GROUPS) * NQ)
        s_shi = sig("small_weights_hi", 1)
        s_slo = sig("small_weights_lo", 1)
        s_init = ctx.enter_context(nc.semaphore("tiles_initialised"))
        s_ghalf = sig("gate_bias_halved", 1)
        s_xstd = sig("x_std", TILES)
        s_xn = sig("x_normalised", TILES)
        s_xt = sig("x_transposed", 2 * TILES)
        s_hhi = sig("h_hi_written", 2 * TILES)
        s_hlo = sig("h_lo_written", 2 * TILES)
        s_job = sig("job_done", NJOBS)
        s_free = [sig(f"bank_free{i}", NJOBS // GBANKS) for i in range(GBANKS)]
        s_small = sig("small_product_copied", TILES)
        s_stage = sig("tile_staged", 3 * TILES)
        s_xg = sig("heads_scaled", 2 * TILES)
        s_cos = sig("tile_times_cos", 3 * TILES)
        s_rinv = sig("heads_rstd", 2 * TILES)
        s_rot = sig("tile_rotated", 3 * TILES)
        s_rott = sig("rotated_transposed", 3 * TILES)
        s_rotc = sig("rotated_copied", 3 * TILES)
        s_idxp = sig("index_logits", len(IDX_STEPS))
        s_relu = sig("index_relu", len(IDX_STEPS))
        s_idx = sig("index_added", len(IDX_STEPS))
        s_vb = sig("v_copied", TILES)
        s_va = sig("va_gelu", TILES)
        s_u = sig("u_gelu", TILES)
        s_wst = sig("ws_transposed", 1)
        s_wsc = sig("ws_copied", 1)
        s_wsz = sig("ws_masked", 1)
        s_lnv = sig("ln_variance", 1)
        s_lnstd = sig("ln_std", 1)
        s_ln = sig("ln_applied", TILES)
        s_mix = sig("mixed", A_GROUPS)
        s_um = sig("u_times_mixed", A_GROUPS)
        s_tanh = sig("tanh_half_z", 8)
        s_zused = sig("tanh_half_z_used", 8)
        s_ya = sig("ya_ready", A_GROUPS)
        s_yahi = sig("ya_hi_written", A_GROUPS)
        s_yalo = sig("ya_lo_written", A_GROUPS)
        s_ga = sig("gate_a", KD)
        s_gb = sig("gate_b", KD)
        s_ma = sig("branch_a_gated", KD)
        s_sum = sig("branches_added", KD)
        s_mhi = sig("merged_hi", KD)
        s_mlo = sig("merged_lo", KD)
        s_qk = sig("scores", len(ATT_STEPS))
        s_max = sig("score_max", len(ATT_STEPS))
        s_exp = sig("exponentials", len(ATT_STEPS))
        s_prob = sig("probs_scaled", len(ATT_STEPS))
        s_pt = sig("probs_transposed", len(ATT_STEPS))
        s_ptc = sig("probs_t_copied", len(ATT_STEPS))
        s_pv = sig("attended", len(ATT_STEPS))
        s_yb = sig("yb_ready", TILES)
        s_ybhi = sig("yb_hi_written", HEADS)
        s_yblo = sig("yb_lo_written", HEADS)
        s_xback = sig("x_reloaded", 16, False)
        s_res = sig("residual_added", 2 * TILES)
        s_out = ctx.enter_context(nc.semaphore("out_stored"))
        s_stash = sig("x_stashed", 16, False)
        s_eye = ctx.enter_context(nc.semaphore("identity_in"))
        vec = Steps(ctx, nc, "vector_steps")
        act_ = Steps(ctx, nc, "scalar_steps")
        poo = Steps(ctx, nc, "gpsimd_steps")

        def seed(engine, *signals):
            for s in signals:
                engine.sem_inc(s.sem, s.per)

        waits_over = ctx.enter_context(nc.semaphore("waits_over"))

        def pause(engine):
            engine.sem_inc(waits_over, 1)

        block = ctx.enter_context(nc.Block())

        def block_cols(b):
            at = sum(P * (c + 1) for c in range(1, b))
            return slice(at, at + P * (b + 1))

        def w_slot(g):
            return g % 2

        def slot_free(layer, g):
            return s_job.at(layer, FIRST_JOB[g - 1] if g >= 2 else FIRST_JOB[g - 1 + len(GROUPS)] - NJOBS)

        def quarters_in(j):
            g = next(i for i in range(len(GROUPS)) if FIRST_JOB[i] <= j < FIRST_JOB[i + 1])
            i, wide = j - FIRST_JOB[g], GROUPS[g][3] // NQ
            if g + 1 == len(GROUPS) or i % wide:
                return []
            return [(g + 1, qt) for qt in (((0,), (1,), (2, 3), ()) if wide == 1 else ((0,), (1,), (2,), (3,)))[i // wide]]

        @block.sync
        def _(sp):
            for t in range(TILES):
                sp.dma_start(x_sb[:, t, :], x[t * P:(t + 1) * P, :]).then_inc(s_x0[t], 16)
            with sp.Fori(0, DEPTH) as layer:
                for g, (name, matrix, col, _) in enumerate(GROUPS):
                    src = dict(w_in=w_in, w_oa=w_oa, w_ob=w_ob, w_out=w_out)[matrix][bass.ds(layer, 1)]
                    for qt in range(NQ):
                        n = g * NQ + qt
                        sp.wait_ge(s_wlo.sem, s_wlo.at(layer, n - RAW + 1))
                        pause(sp)
                        if matrix in ("w_oa", "w_ob"):
                            part = src[:, qt * P:(qt + 1) * P, :].rearrange("a p (c n) -> (a p) c n", c=2)
                        else:
                            part = src[:, 2 * qt * P:(2 * qt + 2) * P, col:col + W512] \
                                .rearrange("a (k p) n -> p (a k) n", p=P)
                        sp.dma_start(w_raw[:, n % RAW], part).then_inc(s_wraw[n % RAW].sem, 16)
            for t in range(TILES):
                sp.wait_ge(s_res.sem, s_res.at(DEPTH - 1, TILES + t + 1))
                sp.dma_start(out[t * P:(t + 1) * P, :], x_sb[:, t, :]).then_inc(s_out, 16)
            sp.wait_ge(s_out, 16 * TILES)

        @block.gpsimd
        def _(pool):
            seed(pool, s_xg, s_cos)
            with pool.Fori(0, DEPTH) as layer:
                l = bass.ds(layer, 1)
                pool.wait_ge(s_mlo.sem, s_mlo.at(layer, 0))
                pause(pool)
                pool.dma_start(norm_bc[:], norm_g[l].to_broadcast([P, D])).then_inc(s_norm.sem, 16)
                pool.dma_start(s_raw[:], w_in[l, :, COL["ik"]:COL["ik"] + SMALL]
                               .rearrange("a (k p) n -> p (a k) n", p=P)).then_inc(s_small_in.sem, 16)
                for dst, src in ((kg_bc, k_norm_g), (qg_bc, q_norm_g), (lng_bc, a_ln_g), (lnb_bc, a_ln_b)):
                    pool.dma_start(dst[:], src[l].to_broadcast([P, dst.shape[1]])).then_inc(s_par.sem, 16)
                pool.dma_start(bs_bc[:], a_bs[l].rearrange("a (g i) -> a g i", g=A_GROUPS)
                               .to_broadcast([P, A_GROUPS, P])).then_inc(s_par.sem, 16)
                pool.dma_start(ws_raw[:], a_ws[l].rearrange("a g i j -> i (a g) j")).then_inc(s_par.sem, 16)
                pool.dma_start(gate_raw[:], gate_b[l].rearrange("a p c -> (a p) c")).then_inc(s_par.sem, 16)
                pool.wait_ge(s_xn.sem, s_xn.at(layer, 2))
                pool.wait_ge(s_res.sem, s_res.at(layer, 0))
                for t in range(TILES):
                    pool.wait_ge(s_x0[t], 16)
                pool.wait_ge(s_const, 16 * 4)
                pause(pool)
                pool.dma_start(out.rearrange("(t p) d -> p t d", p=P), x_sb[:]).then_inc(s_stash.sem, 16)
                pool.wait_ge(s_par.sem, s_par.at(layer, 16 * N_PARAMS))
                def times_cos(n, tile, heads, dim, cos):
                    pool.wait_ge(s_rot.sem, s_rot.at(layer, n))
                    nc.gpsimd.tensor_tensor(
                        rope_a[:, 0:heads * dim].rearrange("p (h d) -> p h d", h=heads),
                        tile, cos.unsqueeze(1).to_broadcast([P, heads, dim]), ALU.mult).then_inc(s_cos.sem, 1)

                for n in range(TILES):
                    pool.wait_ge(s_stage.sem, s_stage.at(layer, n + 1))
                    times_cos(n, stage[:, n % 2, 0:ROT_I].rearrange("p (h d) -> p h d", h=IH + 1), IH + 1, ID, ci[:, n])
                for n in range(2 * TILES):
                    g_bc = kg_bc if n < TILES else qg_bc
                    tile = stage[:, (TILES + n) % 2, 0:HEADS * DH].rearrange("p (h d) -> p h d", h=HEADS)
                    pool.wait_ge(s_rinv.sem, s_rinv.at(layer, n + 1))
                    poo.link(pool, nc.gpsimd.tensor_tensor(
                        tile, tile, rstd[:, HEADS * n:HEADS * n + HEADS].unsqueeze(2).to_broadcast([P, HEADS, DH]),
                        ALU.mult))
                    nc.gpsimd.tensor_tensor(tile, tile, g_bc[:].unsqueeze(1).to_broadcast([P, HEADS, DH]),
                                            ALU.mult).then_inc(s_xg.sem, 1)
                    pool.wait_ge(s_xg.sem, s_xg.at(layer, n + 1))
                    times_cos(TILES + n, tile, HEADS, DH, cq[:, n % TILES])
                pool.wait_ge(s_yblo.sem, s_yblo.at(layer, HEADS))
                pool.wait_ge(s_stash.sem, s_stash.at(layer, 16))
                pause(pool)
                pool.dma_start(x_sb[:], out.rearrange("(t p) d -> p t d", p=P)).then_inc(s_xback.sem, 16)
                pause(pool)
                poo.end_layer(pool)

        @block.tensor
        def _(pe):
            seed(pe, s_job, s_xt, s_rott, s_idxp, s_wst, s_mix, s_qk, s_pt, s_pv)
            pe.wait_ge(s_eye, 16)

            def transpose_x(layer, t):
                pe.wait_ge(s_xn.sem, s_xn.at(layer, t + 1))
                if t >= 2:
                    pe.wait_ge(s_hlo.sem, s_hlo.at(layer, 2 * (t - 1)))
                for half in range(2):
                    dst = bank[3 + 2 * (t % 2) + half]
                    for k in range(4):
                        kk = 4 * half + k
                        last = nc.tensor.transpose(dst[:, k * P:(k + 1) * P], xn[:, t % 2, kk * P:(kk + 1) * P], eye[:])
                    last.then_inc(s_xt.sem, 1)

            def transpose_rotated(layer, n):
                pe.wait_ge(s_rot.sem, s_rot.at(layer, n + 1))
                if n == 0:
                    pe.wait_ge(s_hlo.sem, s_hlo.at(layer, 2 * TILES))
                else:
                    pe.wait_ge(s_rotc.sem, s_rotc.at(layer, n))
                index = n < TILES
                for c in range(4 if n else 0):
                    last = nc.tensor.transpose(bank[5][:, c * P:(c + 1) * P], rot[:, c * P:(c + 1) * P], eye[:])
                if index:
                    last = nc.tensor.transpose(bank[6][:, 0:P], rot[:, IH * ID:IH * ID + 2 * ID], eye[:])
                last.then_inc(s_rott.sem, 1)

            def index_logits(layer, n):
                b, h = IDX_STEPS[n]
                if n < 2:
                    pe.wait_ge(s_rotc.sem, s_rotc.at(layer, TILES))
                else:
                    pe.wait_ge(s_relu.sem, s_relu.at(layer, n - 1))
                half = slice(ID * (h % 2), ID * (h % 2) + ID)
                nc.tensor.matmul(bank[3 + n % 2][:, 0:P * (b + 1)], qi_t[half, h // 2, (b - 1) * P:b * P],
                                 ki_t[half, 0:P * (b + 1)], start=True, stop=True).then_inc(s_idxp.sem, 1)

            def transpose_ws(layer):
                pe.wait_ge(s_par.sem, s_par.at(layer, 16 * N_PARAMS))
                pe.wait_ge(s_rotc.sem, s_rotc.at(layer, 3 * TILES))
                for g in range(A_GROUPS):
                    last = nc.tensor.transpose(bank[5][:, g * P:(g + 1) * P], ws_raw[:, g], eye[:])
                last.then_inc(s_wst.sem, 1)

            def mix(layer, g):
                if g == 0:
                    pe.wait_ge(s_ln.sem, s_ln.at(layer, TILES))
                    pe.wait_ge(s_wsc.sem, s_wsc.at(layer, 1))
                    pe.wait_ge(s_wsz.sem, s_wsz.at(layer, 1))
                    pe.wait_ge(s_relu.sem, s_relu.at(layer, len(IDX_STEPS)))
                for n in range(TILES):
                    last = nc.tensor.matmul(bank[3 + g][:, n * P:(n + 1) * P], v_a[:, n, g * P:(g + 1) * P],
                                            ws_t[:, g], start=True, stop=True)
                last.then_inc(s_mix.sem, 1)

            def attend(layer, i):
                if i >= 2:
                    h, b = ATT_STEPS[i - 2]
                    pe.wait_ge(s_ptc.sem, s_ptc.at(layer, i - 1))
                    if h == 0 and b:
                        pe.wait_ge(s_yb.sem, s_yb.at(layer, b))
                    for c in range(b + 1):
                        last = nc.tensor.matmul(bank[7][:, h * P:(h + 1) * P], v_b[:, c, h * DH:(h + 1) * DH],
                                                probs_t[:, c * P:(c + 1) * P], start=(c == 0), stop=(c == b))
                    last.then_inc(s_pv.sem, 1)
                if 1 <= i <= len(ATT_STEPS):
                    h, b = ATT_STEPS[i - 1]
                    pe.wait_ge(s_prob.sem, s_prob.at(layer, i))
                    if i >= 2:
                        pe.wait_ge(s_ptc.sem, s_ptc.at(layer, i - 1))
                    for c in range(b + 1):
                        last = nc.tensor.transpose(bank[5][:, c * P:(c + 1) * P],
                                                   probs[:, (i - 1) % 2, c * P:(c + 1) * P], eye[:])
                    last.then_inc(s_pt.sem, 1)
                if i < len(ATT_STEPS):
                    h, b = ATT_STEPS[i]
                    if i == 0:
                        pe.wait_ge(s_um.sem, s_um.at(layer, A_GROUPS))
                    if i >= 2:
                        pe.wait_ge(s_max.sem, s_max.at(layer, i - 1))
                    nc.tensor.matmul(bank[3 + i % 2][:, 0:P * (b + 1)], q_t[:, h, b * P:(b + 1) * P],
                                     k_t[:, h, 0:P * (b + 1)], start=True, stop=True).then_inc(s_qk.sem, 1)

            def three_pass(dst, pairs, ready=None):
                for n, (s_h, s_l, m_h, m_l) in enumerate(pairs):
                    if ready:
                        ready(n)
                    nc.tensor.matmul(dst, s_h, m_l, start=(n == 0), stop=False)
                    nc.tensor.matmul(dst, s_l, m_h, start=False, stop=False)
                    last = nc.tensor.matmul(dst, s_h, m_h, start=False, stop=(n == len(pairs) - 1))
                return last

            def job(layer, g, j):
                name = GROUPS[g][0]
                n, i, slot = FIRST_JOB[g] + j, j, w_slot(g)
                dst = bank[n % GBANKS]
                pe.wait_ge(s_free[n % GBANKS].sem, s_free[n % GBANKS].at(layer, n // GBANKS))
                if name in ("oa", "ob"):
                    y_hi, y_lo = (ya_hi, ya_lo) if name == "oa" else (yb_hi, yb_lo)
                    done = s_yalo if name == "oa" else s_yblo
                    pairs = []
                    for k in range(A_GROUPS):
                        c = slice((i % 4) * P, (i % 4 + 1) * P)
                        piece = 2 * k + i // 4
                        pairs.append((w_hi[:, slot, piece, c], w_lo[:, slot, piece, c], y_hi[:, k], y_lo[:, k]))

                    def ready(k):
                        if j == 0:
                            pe.wait_ge(s_wlo.sem, s_wlo.at(layer, NQ * g + k + 1))
                            pe.wait_ge(done.sem, done.at(layer, k + 1))
                else:
                    tok = slice(j * P, (j + 1) * P)
                    if name in TOKEN_MAJOR:
                        pairs = [(h_hi[:, k, tok], h_lo[:, k, tok], w_hi[:, slot, k], w_lo[:, slot, k])
                                 for k in range(KD)]
                    else:
                        pairs = [(w_hi[:, slot, k, tok], w_lo[:, slot, k, tok], h_hi[:, k], h_lo[:, k])
                                 for k in range(KD)]
                    def ready(k):
                        if name == "iq" and k % (KD // 2) == 0:
                            pe.wait_ge(s_hlo.sem, s_hlo.at(layer, 2 * j + k // (KD // 2) + 1))
                        if name == "iq" and k == KD // 2 and j + 1 < TILES:
                            transpose_x(layer, j + 1)
                        if j == 0 and k % 2 == 0:
                            pe.wait_ge(s_wlo.sem, s_wlo.at(layer, NQ * g + k // 2 + 1))
                        if name == "out" and n == JOB_OUT[0]:
                            pe.wait_ge(s_mlo.sem, s_mlo.at(layer, k + 1))
                last = three_pass(dst[:], pairs, ready)
                if name == "iq":
                    if j == 0:
                        pe.wait_ge(s_slo.sem, s_slo.at(layer, 1))
                    pe.wait_ge(s_small.sem, s_small.at(layer, j))
                    tok = slice(j * P, (j + 1) * P)
                    last = three_pass(bank[7][:, j * SMALL:(j + 1) * SMALL],
                                      [(h_hi[:, k, tok], h_lo[:, k, tok], s_hi[:, k], s_lo[:, k]) for k in range(KD)])
                last.then_inc(s_job.sem, 1)

            with pe.Fori(0, DEPTH) as layer:
                transpose_x(layer, 0)
                for g in range(len(GROUPS)):
                    for j in range(GROUPS[g][3]):
                        n = FIRST_JOB[g] + j
                        job(layer, g, j)
                        if n in AFTER_QI:
                            transpose_rotated(layer, AFTER_QI[n])
                        if n in AFTER_K:
                            transpose_rotated(layer, TILES + AFTER_K[n])
                        if n in AFTER_Q:
                            transpose_rotated(layer, 2 * TILES + AFTER_Q[n])
                        for step in AFTER_IDX.get(n, []):
                            index_logits(layer, step)
                        if n == AFTER_WS:
                            transpose_ws(layer)
                        for group in AFTER_MIX.get(n, []):
                            mix(layer, group)
                        if n in AFTER_ATT:
                            attend(layer, AFTER_ATT[n])

        @block.scalar
        def _(act):
            seed(act, s_whi, s_shi, s_xstd, s_hhi, s_small, s_stage, s_rotc, s_relu, s_vb, s_va, s_u, s_wsc,
                 s_lnstd, s_tanh, s_yahi, s_ga, s_gb, s_mhi, s_exp, s_ptc, s_ybhi, *s_free)

            act.dma_start(eye[:], ident).then_inc(s_eye, 16)
            for dst, src in ((ci, cos_i), (si, sin_i), (cq, cos_qk), (sq, sin_qk)):
                act.dma_start(dst[:], src).then_inc(s_const, 16)

            def rounded(layer, g, qt):
                n = g * NQ + qt
                act.wait_ge(s_wraw[n % RAW].sem, s_wraw[n % RAW].at(layer, 16 * (n // RAW + 1)))
                act.wait_ge(s_job.sem, slot_free(layer, g))
                nc.scalar.activation(w_hi[:, w_slot(g), 2 * qt:2 * qt + 2], w_raw[:, n % RAW], ACT.Copy) \
                    .then_inc(s_whi.sem, 1)

            def root(layer, dst, src, scale=1.0):
                return nc.scalar.activation(dst, src, ACT.Sqrt, bias=eps[:], scale=scale)

            def head_std(layer, n, src):
                c = HEADS * n
                for h in range(HEADS):
                    act_.mark(nc.scalar.activation(bank[7][:, h * DH:(h + 1) * DH], src[:, h * DH:(h + 1) * DH], ACT.Square,
                                                   scale=DH ** -0.5, accum_out=ms[:, c + h:c + h + 1]))
                act_.join(act)
                act_.mark(root(layer, std[:, c:c + HEADS], ms[:, c:c + HEADS]))

            def evacuate(layer, n):
                src, free = bank[n % GBANKS], s_free[n % GBANKS]
                if n in JOB_OA + JOB_OB + JOB_OUT:
                    return
                act.wait_ge(s_job.sem, s_job.at(layer, n + 1))
                if n in JOB_IQ:
                    t = n - JOB_IQ[0]
                    act.wait_ge(s_rot.sem, s_rot.at(layer, t - 1))
                    if t == 0:
                        act.wait_ge(s_zused.sem, s_zused.at(layer, 0))
                    nc.scalar.activation(stage[:, t % 2, 0:IH * ID], src[:], ACT.Copy).then_inc(free.sem, 1)
                    act_.mark(nc.scalar.activation(stage[:, t % 2, IH * ID:IH * ID + SMALL],
                                                   bank[7][:, t * SMALL:(t + 1) * SMALL], ACT.Copy))
                    act_.join(act)
                    act.sem_inc(s_small.sem, 1)
                    act.sem_inc(s_stage.sem, 1)
                elif n in JOB_K or n in JOB_Q:
                    t = n - JOB_K[0]
                    act.wait_ge(s_rot.sem, s_rot.at(layer, TILES + t - 1))
                    head_std(layer, t, src)
                    act_.mark(nc.scalar.activation(stage[:, (TILES + t) % 2, 0:HEADS * DH], src[:], ACT.Copy))
                    act_.join(act)
                    act.sem_inc(free.sem, 1)
                    act.sem_inc(s_stage.sem, 1)
                elif n in JOB_VB:
                    t = n - JOB_VB[0]
                    act_.mark(nc.scalar.activation(v_b[:, t], src[:], ACT.Copy))
                    act_.join(act)
                    act.sem_inc(free.sem, 1)
                    act.sem_inc(s_vb.sem, 1)
                elif n in JOB_VA or n in JOB_U:
                    dst, done, t = (v_a, s_va, n - JOB_VA[0]) if n in JOB_VA else (u_a, s_u, n - JOB_U[0])
                    act_.mark(nc.scalar.activation(dst[:, t], src[:], ACT.Gelu_apprx_tanh))
                    act_.join(act)
                    act.sem_inc(free.sem, 1)
                    act.sem_inc(done.sem, 1)
                elif n in JOB_ZB or n in JOB_ZA:
                    t = n - JOB_ZB[0]
                    if n == JOB_ZB[0]:
                        act.wait_ge(s_lnv.sem, s_lnv.at(layer, 1))
                        root(layer, ln_std[:], mv[:, :, 1]).then_inc(s_lnstd.sem, 1)
                    act.wait_ge(s_zused.sem, s_zused.at(layer, t - 1))
                    if t == 0:
                        act.wait_ge(s_rot.sem, s_rot.at(layer, 3 * TILES))
                    nc.scalar.activation(t_half[:, t % 2], src[:], ACT.Tanh, scale=0.5).then_inc(s_tanh.sem, 1)
                elif n in JOB_GA or n in JOB_GB:
                    dst, done, d, c = (g_a, s_ga, n - JOB_GA[0], 0) if n in JOB_GA else (g_b, s_gb, n - JOB_GB[0], KD)
                    if n == JOB_GA[0]:
                        act.wait_ge(s_mix.sem, s_mix.at(layer, A_GROUPS))
                        act.wait_ge(s_ghalf.sem, s_ghalf.at(layer, 1))
                    if n == JOB_GA[4]:
                        act.wait_ge(s_yalo.sem, s_yalo.at(layer, A_GROUPS))
                    if n == JOB_GB[0]:
                        act.wait_ge(s_job.sem, s_job.at(layer, JOB_OA[-1] + 1))
                    act_.mark(nc.scalar.activation(dst[:, d], src[:], ACT.Tanh, scale=0.5,
                                                   bias=gate_half[:, c + d:c + d + 1]))
                    act_.join(act)
                    act.sem_inc(free.sem, 1)
                    act.sem_inc(done.sem, 1)

            def beside(layer, n):
                for after, base in ((AFTER_QI, 0), (AFTER_K, TILES), (AFTER_Q, 2 * TILES)):
                    if n in after:
                        t = after[n]
                        act.wait_ge(s_rott.sem, s_rott.at(layer, base + t + 1))
                        four = bank[5][:].rearrange("p (c q) -> p c q", c=4)
                        if base == 0:
                            if t == 0:
                                act.wait_ge(s_stash.sem, s_stash.at(layer, 16))
                                act.wait_ge(s_xt.sem, s_xt.at(layer, 2 * TILES))
                            if t:
                                act_.mark(nc.scalar.activation(qi_t[:, :, (t - 1) * P:t * P], four, ACT.Copy))
                            act_.mark(nc.scalar.activation(ki_t[:, t * P:(t + 1) * P], bank[6][:, 0:P], ACT.Copy))
                        else:
                            dst = k_t if base == TILES else q_t
                            act_.mark(nc.scalar.activation(dst[:, :, t * P:(t + 1) * P], four, ACT.Copy))
                        act_.join(act)
                        act.sem_inc(s_rotc.sem, 1)
                for i in AFTER_IDX.get(n, []):
                    b, h = IDX_STEPS[i]
                    w = P * (b + 1)
                    act.wait_ge(s_idxp.sem, s_idxp.at(layer, i + 1))
                    if i >= 2:
                        act.wait_ge(s_idx.sem, s_idx.at(layer, i - 1))
                    nc.scalar.activation(probs[:, i % 2, 0:w], bank[3 + i % 2][:, 0:w], ACT.Relu).then_inc(s_relu.sem, 1)
                if n == AFTER_WS:
                    act.wait_ge(s_wst.sem, s_wst.at(layer, 1))
                    four = bank[5][:].rearrange("p (c q) -> p c q", c=A_GROUPS)
                    act_.mark(nc.scalar.activation(ws_t[0:CHUNK], four[0:CHUNK], ACT.Copy))
                    act_.mark(nc.scalar.activation(ws_t[CHUNK:P, :, CHUNK:P], four[CHUNK:P, :, CHUNK:P], ACT.Copy))
                    act_.join(act)
                    act.sem_inc(s_wsc.sem, 1)
                if n - 1 in JOB_ZA:
                    c = n - 1 - JOB_ZA[0]
                    act.wait_ge(s_ya.sem, s_ya.at(layer, c + 1))
                    nc.scalar.activation(ya_hi[:, c], u_a[:, c], ACT.Copy).then_inc(s_yahi.sem, 1)
                if n in AFTER_ATT:
                    i = AFTER_ATT[n]
                    if i >= 1 and i <= len(ATT_STEPS):
                        b = ATT_STEPS[i - 1][1]
                        w = P * (b + 1)
                        act.wait_ge(s_pt.sem, s_pt.at(layer, i))
                        if i >= 2:
                            act.wait_ge(s_pv.sem, s_pv.at(layer, i - 1))
                        nc.scalar.activation(probs_t[:, 0:w], bank[5][:, 0:w], ACT.Copy).then_inc(s_ptc.sem, 1)
                    if i < len(ATT_STEPS):
                        w = P * (ATT_STEPS[i][1] + 1)
                        act.wait_ge(s_max.sem, s_max.at(layer, i + 1))
                        act_.mark(nc.scalar.activation(probs[:, i % 2, 0:w], probs[:, i % 2, 0:w], ACT.Exp,
                                                       bias=neg_max[:, i:i + 1], scale=ATT_SCALE,
                                                       accum_out=row_sum[:, i:i + 1]))
                        act_.join(act)
                        act.sem_inc(s_exp.sem, 1)
                if n in SPLIT_YB:
                    h = SPLIT_YB[n]
                    act.wait_ge(s_yb.sem, s_yb.at(layer, TILES))
                    nc.scalar.activation(yb_hi[:, h], z_b[:, h], ACT.Copy).then_inc(s_ybhi.sem, 1)
                if n in JOB_OB:
                    d = n - JOB_OB[0]
                    act.wait_ge(s_sum.sem, s_sum.at(layer, d + 1))
                    if d == 0:
                        act.wait_ge(s_job.sem, s_job.at(layer, JOB_GB[-1] + 1))
                    nc.scalar.activation(h_hi[:, d], g_b[:, d], ACT.Copy, scale=0.5).then_inc(s_mhi.sem, 1)

            def x_std(layer, t):
                c = 2 * TILES * HEADS + t
                act.wait_ge(s_res.sem, s_res.at(layer, t + 1 - TILES))
                act.wait_ge(s_x0[t], 16)
                if t == 0:
                    act.wait_ge(s_max.sem, s_max.at(layer, 0))
                act_.link(act, nc.scalar.activation(score[:, 0:D], x_sb[:, t], ACT.Square, scale=D ** -0.5,
                                                    accum_out=ms[:, c:c + 1]))
                root(layer, std[:, c:c + 1], ms[:, c:c + 1]).then_inc(s_xstd.sem, 1)

            def h_rounded(layer, t):
                act.wait_ge(s_job.sem, s_job.at(layer, JOB_OUT[TILES + t] + 1 - NJOBS))
                for half in range(2):
                    act.wait_ge(s_xt.sem, s_xt.at(layer, 2 * t + half + 1))
                    nc.scalar.activation(h_hi[:, 4 * half:4 * half + 4, t * P:(t + 1) * P],
                                         bank[3 + 2 * (t % 2) + half][:].rearrange("p (c q) -> p c q", c=4),
                                         ACT.Copy).then_inc(s_hhi.sem, 1)

            act.wait_ge(s_init, 1)
            with act.Fori(0, DEPTH) as layer:
                nc.scalar.preload_act_table(ACT.Sqrt)
                x_std(layer, 0)
                rounded(layer, 0, 0)
                x_std(layer, 1)
                rounded(layer, 0, 1)
                h_rounded(layer, 0)
                x_std(layer, 2)
                rounded(layer, 0, 2)
                rounded(layer, 0, 3)
                x_std(layer, 3)
                act.wait_ge(s_small_in.sem, s_small_in.at(layer, 16))
                nc.scalar.activation(s_hi[:], s_raw[:], ACT.Copy).then_inc(s_shi.sem, 1)
                for n in range(NJOBS):
                    if n + 1 < TILES:
                        h_rounded(layer, n + 1)
                    for g, qt in quarters_in(n):
                        rounded(layer, g, qt)
                    evacuate(layer, n)
                    beside(layer, n)
                pause(act)
                act_.end_layer(act)

        @block.vector
        def _(dve):
            seed(dve, s_wlo, s_slo, s_ghalf, s_xn, s_hlo, s_rinv, s_rot, s_idx, s_wsz, s_lnv, s_ln, s_um, s_zused,
                 s_ya, s_yalo, s_ma, s_sum, s_mlo, s_max, s_prob, s_yb, s_yblo, s_res)
            vec.mark(nc.vector.memset(diag[:], 0.0))
            vec.join(dve)
            vec.mark(nc.vector.memset(diag[0:CHUNK, CHUNK:P], FILL))
            vec.mark(nc.vector.memset(eps[:], EPS))
            vec.join(dve)
            dve.sem_inc(s_init, 1)
            vec.end_layer(dve)

            def remainder(layer, g, qt):
                n = g * NQ + qt
                dve.wait_ge(s_whi.sem, s_whi.at(layer, n + 1))
                nc.vector.tensor_tensor(w_lo[:, w_slot(g), 2 * qt:2 * qt + 2], w_raw[:, n % RAW],
                                        w_hi[:, w_slot(g), 2 * qt:2 * qt + 2].bitcast(F32), ALU.subtract) \
                    .then_inc(s_wlo.sem, 1)

            def rotate(layer, n, tile, heads, dim, sin):
                w, half = heads * dim, dim // 2
                src = tile[:, 0:w].rearrange("p (h d) -> p h d", h=heads)
                b = rope_b[:, 0:w].rearrange("p (h d) -> p h d", h=heads)
                for lo, hi in ((slice(0, half), slice(half, dim)), (slice(half, dim), slice(0, half))):
                    vec.mark(nc.vector.tensor_tensor(b[:, :, lo], src[:, :, hi],
                                                     sin[:, lo].unsqueeze(1).to_broadcast([P, heads, half]), ALU.mult))
                vec.join(dve)
                dve.wait_ge(s_cos.sem, s_cos.at(layer, n + 1))
                return nc.vector.tensor_tensor(rot[:, 0:w], rope_a[:, 0:w], rope_b[:, 0:w], ALU.add)

            def rotated(layer, n):
                dve.wait_ge(s_rott.sem, s_rott.at(layer, n))
                if n < TILES:
                    dve.wait_ge(s_stage.sem, s_stage.at(layer, n + 1))
                    tile = stage[:, n % 2]
                    vec.mark(nc.vector.tensor_scalar(head_w[:, n], tile[:, ROT_I:ROT_I + IH], IDX_SCALE, None, ALU.mult))
                    vec.mark(rotate(layer, n, tile, IH + 1, ID, si[:, n]))
                    vec.join(dve)
                    nc.vector.tensor_copy(rot[:, ROT_I:ROT_I + ID], rot[:, IH * ID:ROT_I]).then_inc(s_rot.sem, 1)
                else:
                    m = n - TILES
                    dve.wait_ge(s_xg.sem, s_xg.at(layer, m + 1))
                    rotate(layer, n, stage[:, n % 2], HEADS, DH, sq[:, m % TILES]).then_inc(s_rot.sem, 1)

            def index_add(layer, i):
                b, h = IDX_STEPS[i]
                cols, w = block_cols(b), P * (b + 1)
                weight = head_w[:, b, h:h + 1]
                dve.wait_ge(s_relu.sem, s_relu.at(layer, i + 1))
                if h == 0:
                    op = nc.vector.tensor_scalar(score[:, cols], probs[:, i % 2, 0:w], weight, None, ALU.mult)
                else:
                    op = nc.vector.scalar_tensor_tensor(score[:, cols], probs[:, i % 2, 0:w], weight, score[:, cols],
                                                        ALU.mult, ALU.add)
                op.then_inc(s_idx.sem, 1)
                dve.wait_ge(s_idx.sem, s_idx.at(layer, i + 1))
                if h == IH - 1:
                    last = score[:, cols.stop - P:cols.stop]
                    vec.link(dve, nc.vector.tensor_tensor(last, last, diag[:], ALU.add))

            def topk_round(b, r):
                s = score[:, block_cols(b)]
                vec.link(dve, nc.vector.max(top8[:], s))
                vec.link(dve, nc.vector.match_replace(s, top8[:], s, TAKEN))
                if r == ROUNDS - 1:
                    vec.link(dve, nc.vector.tensor_scalar(s, s, TAKEN, FILL, ALU.not_equal, ALU.mult))

            def attention_scale(layer, i):
                w = P * (ATT_STEPS[i][1] + 1)
                dve.wait_ge(s_exp.sem, s_exp.at(layer, i + 1))
                vec.link(dve, nc.vector.reciprocal(row_inv[:, i:i + 1], row_sum[:, i:i + 1]))
                nc.vector.tensor_scalar(probs[:, i % 2, 0:w], probs[:, i % 2, 0:w], row_inv[:, i:i + 1], None,
                                        ALU.mult).then_inc(s_prob.sem, 1)

            def attention_max(layer, i):
                b = ATT_STEPS[i][1]
                w = P * (b + 1)
                mask = score[:, block_cols(b)] if b else diag[:]
                dve.wait_ge(s_qk.sem, s_qk.at(layer, i + 1))
                if i >= 2:
                    dve.wait_ge(s_pt.sem, s_pt.at(layer, i - 1))
                pause(dve)
                vec.link(dve, nc.vector.tensor_tensor_reduce(
                    out=probs[:, i % 2, 0:w], in0=bank[3 + i % 2][:, 0:w], in1=mask, scale=1.0, scalar=2 * FILL,
                    op0=ALU.add, op1=ALU.max, accum_out=row_max[:, i:i + 1]))
                nc.vector.tensor_scalar(neg_max[:, i:i + 1], row_max[:, i:i + 1], -ATT_SCALE, None,
                                        ALU.mult).then_inc(s_max.sem, 1)

            def merged_lo(layer, d):
                dve.wait_ge(s_mhi.sem, s_mhi.at(layer, d + 1))
                nc.vector.scalar_tensor_tensor(h_lo[:, d], g_b[:, d], 0.5, h_hi[:, d].bitcast(F32),
                                               ALU.mult, ALU.subtract).then_inc(s_mlo.sem, 1)

            def evacuate(layer, n):
                src, free = bank[n % GBANKS], s_free[n % GBANKS]
                if n in JOB_K or n in JOB_Q:
                    m = n - JOB_K[0]
                    c = HEADS * m
                    dve.wait_ge(s_stage.sem, s_stage.at(layer, TILES + m + 1))
                    nc.vector.reciprocal(rstd[:, c:c + HEADS], std[:, c:c + HEADS]).then_inc(s_rinv.sem, 1)
                elif n in JOB_VA:
                    t = n - JOB_VA[0]
                    dve.wait_ge(s_va.sem, s_va.at(layer, t + 1))
                    vec.link(dve, nc.vector.bn_stats(bn[:, t], v_a[:, t]))
                    op = nc.vector.bn_aggr(mv[:, t], bn[:, t])
                    if t < TILES - 1:
                        vec.mark(op)
                    else:
                        vec.link(dve, op)
                        dve.sem_inc(s_lnv.sem, 1)
                elif n in JOB_ZB:
                    c = n - JOB_ZB[0]
                    dve.wait_ge(s_tanh.sem, s_tanh.at(layer, c + 1))
                    if c == 0:
                        dve.wait_ge(s_idxp.sem, s_idxp.at(layer, len(IDX_STEPS)))
                    vec.link(dve, nc.vector.scalar_tensor_tensor(z_b[:, c], t_half[:, c % 2], 1.0, src[:],
                                                                 ALU.add, ALU.mult))
                    dve.sem_inc(free.sem, 1)
                    dve.sem_inc(s_zused.sem, 1)
                elif n in JOB_ZA:
                    c = n - JOB_ZA[0]
                    dve.wait_ge(s_tanh.sem, s_tanh.at(layer, 4 + c + 1))
                    vec.link(dve, nc.vector.scalar_tensor_tensor(silu_z[:], t_half[:, c % 2], 1.0, src[:],
                                                                 ALU.add, ALU.mult))
                    dve.sem_inc(free.sem, 1)
                    dve.sem_inc(s_zused.sem, 1)
                    vec.link(dve, nc.vector.scalar_tensor_tensor(u_a[:, c], silu_z[:], SILU_HALF, u_a[:, c],
                                                                 ALU.mult, ALU.mult))
                    dve.sem_inc(s_ya.sem, 1)
                elif n in JOB_OA:
                    d = n - JOB_OA[0]
                    dve.wait_ge(s_job.sem, s_job.at(layer, n + 1))
                    dve.wait_ge(s_ga.sem, s_ga.at(layer, d + 1))
                    vec.link(dve, nc.vector.scalar_tensor_tensor(g_a[:, d], g_a[:, d], 1.0, src[:], ALU.add, ALU.mult))
                    dve.sem_inc(free.sem, 1)
                    dve.sem_inc(s_ma.sem, 1)
                elif n in JOB_OB:
                    d = n - JOB_OB[0]
                    dve.wait_ge(s_job.sem, s_job.at(layer, n + 1))
                    dve.wait_ge(s_gb.sem, s_gb.at(layer, d + 1))
                    vec.link(dve, nc.vector.scalar_tensor_tensor(g_b[:, d], g_b[:, d], 1.0, src[:], ALU.add, ALU.mult))
                    dve.sem_inc(free.sem, 1)
                    nc.vector.tensor_tensor(g_b[:, d], g_b[:, d], g_a[:, d], ALU.add).then_inc(s_sum.sem, 1)
                    if d:
                        merged_lo(layer, d - 1)
                    if d == KD - 1:
                        merged_lo(layer, d)
                elif n in JOB_OUT:
                    i = n - JOB_OUT[0]
                    t, half = i % TILES, i // TILES
                    dve.wait_ge(s_job.sem, s_job.at(layer, n + 1))
                    if i == 0:
                        dve.wait_ge(s_xback.sem, s_xback.at(layer, 16))
                    part = x_sb[:, t, half * W512:(half + 1) * W512]
                    vec.link(dve, nc.vector.tensor_tensor(part, part, src[:], ALU.add))
                    dve.sem_inc(free.sem, 1)
                    dve.sem_inc(s_res.sem, 1)

            def ln_apply(layer, t):
                tile = v_a[:, t]
                vec.link(dve, nc.vector.tensor_scalar(tile, tile, mv[:, t, 0:1], ln_rstd[:, t:t + 1],
                                                      ALU.subtract, ALU.mult))
                vec.link(dve, nc.vector.tensor_tensor(tile, tile, lng_bc[:], ALU.mult))
                nc.vector.tensor_tensor(tile, tile, lnb_bc[:], ALU.add).then_inc(s_ln.sem, 1)

            def beside(layer, n):
                for i in AFTER_IDX.get(n, []):
                    index_add(layer, i)
                if n == JOB_VB[0]:
                    nc.vector.memset(ws_t[CHUNK:P, :, 0:CHUNK], 0.0).then_inc(s_wsz.sem, 1)
                    dve.wait_ge(s_par.sem, s_par.at(layer, 16 * N_PARAMS))
                    nc.vector.tensor_scalar(gate_half[:], gate_raw[:], 0.5, None, ALU.mult).then_inc(s_ghalf.sem, 1)
                if n == JOB_ZB[0]:
                    dve.wait_ge(s_par.sem, s_par.at(layer, 16 * N_PARAMS))
                    dve.wait_ge(s_lnstd.sem, s_lnstd.at(layer, 1))
                    vec.link(dve, nc.vector.reciprocal(ln_rstd[:], ln_std[:]))
                for t in LN_TILES.get(n, []):
                    ln_apply(layer, t)
                for g in AFTER_MIX.get(n, []):
                    dve.wait_ge(s_mix.sem, s_mix.at(layer, g + 1))
                    dve.wait_ge(s_u.sem, s_u.at(layer, TILES))
                    m = bank[3 + g][:].rearrange("p (n i) -> p n i", n=TILES)
                    biased = um[:, 0:SEQ].rearrange("p (n i) -> p n i", n=TILES)
                    vec.link(dve, nc.vector.tensor_tensor(biased, m, bs_bc[:, g].unsqueeze(1).to_broadcast([P, TILES, P]),
                                                          ALU.add))
                    vec.link(dve, nc.vector.tensor_tensor(u_a[:, g], um[:, 0:SEQ], u_a[:, g], ALU.mult))
                    dve.sem_inc(s_um.sem, 1)
                if n - 1 in JOB_ZA:
                    c = n - 1 - JOB_ZA[0]
                    dve.wait_ge(s_yahi.sem, s_yahi.at(layer, c + 1))
                    nc.vector.tensor_tensor(ya_lo[:, c], u_a[:, c], ya_hi[:, c].bitcast(F32), ALU.subtract) \
                        .then_inc(s_yalo.sem, 1)
                if n in AFTER_ATT:
                    i = AFTER_ATT[n]
                    if i < len(ATT_STEPS):
                        attention_max(layer, i)
                    if i >= 2 and ATT_STEPS[i - 2][0] == HEADS - 1:
                        b = ATT_STEPS[i - 2][1]
                        dve.wait_ge(s_pv.sem, s_pv.at(layer, i - 1))
                        y = z_b[:, :, b * P:(b + 1) * P]
                        nc.vector.scalar_tensor_tensor(y, y, SILU_HALF, bank[7][:].rearrange("p (h q) -> p h q", h=HEADS),
                                                       ALU.mult, ALU.mult).then_inc(s_yb.sem, 1)
                    if i < len(ATT_STEPS):
                        attention_scale(layer, i)
                if n in SPLIT_YB:
                    h = SPLIT_YB[n]
                    dve.wait_ge(s_ybhi.sem, s_ybhi.at(layer, h + 1))
                    nc.vector.tensor_tensor(yb_lo[:, h], z_b[:, h], yb_hi[:, h].bitcast(F32), ALU.subtract) \
                        .then_inc(s_yblo.sem, 1)

            def x_normalised(layer, t):
                c = 2 * TILES * HEADS + t
                dve.wait_ge(s_xstd.sem, s_xstd.at(layer, t + 1))
                vec.link(dve, nc.vector.reciprocal(rstd[:, c:c + 1], std[:, c:c + 1]))
                if t >= 2:
                    dve.wait_ge(s_xt.sem, s_xt.at(layer, 2 * (t - 1)))
                nc.vector.scalar_tensor_tensor(xn[:, t % 2], x_sb[:, t], rstd[:, c:c + 1], norm_bc[:],
                                               ALU.mult, ALU.mult).then_inc(s_xn.sem, 1)

            def h_remainder(layer, t):
                for half in range(2):
                    dve.wait_ge(s_hhi.sem, s_hhi.at(layer, 2 * t + half + 1))
                    dst = slice(4 * half, 4 * half + 4), slice(t * P, (t + 1) * P)
                    nc.vector.tensor_tensor(h_lo[:, dst[0], dst[1]],
                                            bank[3 + 2 * (t % 2) + half][:].rearrange("p (c q) -> p c q", c=4),
                                            h_hi[:, dst[0], dst[1]].bitcast(F32), ALU.subtract) \
                        .then_inc(s_hlo.sem, 1)

            dve.wait_ge(s_const, 16 * 4)
            with dve.Fori(0, DEPTH) as layer:
                dve.wait_ge(s_norm.sem, s_norm.at(layer, 16))
                x_normalised(layer, 0)
                remainder(layer, 0, 0)
                x_normalised(layer, 1)
                h_remainder(layer, 0)
                for qt in range(1, NQ):
                    remainder(layer, 0, qt)
                dve.wait_ge(s_shi.sem, s_shi.at(layer, 1))
                nc.vector.tensor_tensor(s_lo[:], s_raw[:], s_hi[:].bitcast(F32), ALU.subtract).then_inc(s_slo.sem, 1)
                done = {b: 0 for b in range(1, TILES)}
                for n in range(NJOBS):
                    if n + 1 < TILES:
                        h_remainder(layer, n + 1)
                    if n + 2 < TILES:
                        x_normalised(layer, n + 2)
                    for g, qt in quarters_in(n):
                        remainder(layer, g, qt)
                    if n >= 1 and n - 1 in JOB_IQ + JOB_K + JOB_Q:
                        rotated(layer, n - 1)
                    evacuate(layer, n)
                    beside(layer, n)
                    for s, b, count in TOPK_SLOTS:
                        if s == n:
                            pause(dve)
                        for _ in range(min(count, ROUNDS - done[b]) if s == n else 0):
                            topk_round(b, done[b])
                            done[b] += 1
                assert all(v == ROUNDS for v in done.values())
                pause(dve)
                vec.end_layer(dve)


def rope_tables(dim):
    inv = (ROPE_THETA ** (-np.arange(0, dim, 2, dtype=np.float64) / dim)).astype(np.float32)
    ang = np.arange(SEQ, dtype=np.float32)[:, None] * inv[None, :]
    cos, sin = np.cos(ang), np.sin(ang)
    lay = lambda a: np.ascontiguousarray(a.astype(np.float32).reshape(TILES, P, dim).transpose(1, 0, 2))
    return lay(np.concatenate([cos, cos], 1)), lay(np.concatenate([-sin, sin], 1))


def kernel(x, norm_g, w_in, gate_b, a_ln_g, a_ln_b, a_ws, a_bs, q_norm_g, k_norm_g, w_oa, w_ob, w_out):
    import concourse.bacc as bacc
    from concourse.bass_utils import run_bass_kernel_spmd

    cos_qk, sin_qk = rope_tables(DH)
    cos_i, sin_i = rope_tables(ID)
    gate = np.asarray(gate_b).reshape(DEPTH, 2, KD, P).transpose(0, 3, 1, 2).reshape(DEPTH, P, 2 * KD)
    arrays = dict(x=np.asarray(x).reshape(SEQ, D), norm_g=norm_g, w_in=w_in, gate_b=gate, a_ln_g=a_ln_g,
                  a_ln_b=a_ln_b, a_ws=a_ws, a_bs=np.asarray(a_bs).reshape(DEPTH, A_GROUPS * P), q_norm_g=q_norm_g,
                  k_norm_g=k_norm_g, w_oa=w_oa, w_ob=w_ob, w_out=w_out, ident=np.eye(P, dtype=np.float32),
                  cos_qk=cos_qk, sin_qk=sin_qk, cos_i=cos_i, sin_i=sin_i)
    arrays = {k: np.ascontiguousarray(v) for k, v in arrays.items()}
    nc = bacc.Bacc("TRN2", target_bir_lowering=False, num_devices=1)
    aps = {k: nc.dram_tensor(f"in_{k}", v.shape, F32, kind="ExternalInput").ap() for k, v in arrays.items()}
    out = nc.dram_tensor("out", (SEQ, D), F32, kind="ExternalOutput").ap()
    trunk(nc, **aps, out=out)
    r = run_bass_kernel_spmd(nc, [{f"in_{k}": v for k, v in arrays.items()}], core_ids=[0])
    return r.results[0]["out"].reshape(1, SEQ, D)
```

```python
from contextlib import ExitStack

import concourse.bass as bass
import numpy as np
from concourse import mybir
from concourse.alu_op_type import AluOpType as ALU

F32 = mybir.dt.float32
F32R = mybir.dt.float32r
ACT = mybir.ActivationFunctionType
AX = mybir.AxisListType

P = 128
DEPTH, SEQ, D = 2, 512, 1024
CHUNK = 64
EPS = 1e-6
ROPE_THETA = 10000.0
A_WIDTH, A_GROUPS = 512, 4
HEADS, DH = 4, 128
IH, ID = 8, 64
TOPK = min(256, SEQ // 4)
SPLITS = dict(u=A_WIDTH, va=A_WIDTH, za=A_WIDTH, q=HEADS * DH, k=HEADS * DH, vb=HEADS * DH, zb=HEADS * DH,
              iq=IH * ID, ik=ID, iw=IH, ga=D, gb=D)
COL = dict(zip(SPLITS, np.cumsum([0] + list(SPLITS.values())[:-1]).tolist()))
IN_WIDTH = sum(SPLITS.values())

TILES = SEQ // P
ORDER = [*range(1, TILES), 0]
assert TOPK >= P
KD = D // P
W512 = 512
SMALL = ID + IH
INDEX = IH * ID + SMALL
ROT_I = (IH + 1) * ID
ATT_SCALE = DH ** -0.5
IDX_SCALE = ID ** -0.5 * IH ** -0.5
FILL = -(2.0 ** 126)
TAKEN = -(2.0 ** 127)
SILU_HALF = 0.5

GROUPS = [
    ("iq", "w_in", COL["iq"], 4), ("k", "w_in", COL["k"], 4), ("q", "w_in", COL["q"], 4),
    ("vb", "w_in", COL["vb"], 4), ("va", "w_in", COL["va"], 4), ("u", "w_in", COL["u"], 4),
    ("zb", "w_in", COL["zb"], 4), ("za", "w_in", COL["za"], 4),
    ("ga", "w_in", COL["ga"], 4), ("ga", "w_in", COL["ga"] + W512, 4),
    ("oa", "w_oa", 0, 8),
    ("gb", "w_in", COL["gb"], 4), ("gb", "w_in", COL["gb"] + W512, 4),
    ("ob", "w_ob", 0, 8),
    ("out", "w_out", 0, 4), ("out", "w_out", W512, 4),
]
N_PARAMS = 5
TOKEN_MAJOR = {"iq", "k", "q", "vb", "va", "out"}
FIRST_JOB = np.cumsum([0] + [g[3] for g in GROUPS]).tolist()
NJOBS = FIRST_JOB[-1]
NQ = 4
RAW = 4
WARM_UP = 20
GBANKS = 3
assert NJOBS % GBANKS == 0 and (len(GROUPS) * NQ) % RAW == 0


def jobs_of(name):
    return [FIRST_JOB[g] + j for g in range(len(GROUPS)) if GROUPS[g][0] == name for j in range(GROUPS[g][3])]


JOB_IQ, JOB_K, JOB_Q, JOB_VB, JOB_VA, JOB_U, JOB_ZB, JOB_ZA, JOB_GA, JOB_OA, JOB_GB, JOB_OB, JOB_OUT = (
    jobs_of(n) for n in ("iq", "k", "q", "vb", "va", "u", "zb", "za", "ga", "oa", "gb", "ob", "out"))

AFTER_QI = {JOB_IQ[t] + 2: t for t in range(TILES)}
AFTER_K = {JOB_K[t] + 2: t for t in range(TILES)}
AFTER_Q = {JOB_Q[t] + 2: t for t in range(TILES)}
IDX_STEPS = [(b, h) for b in range(1, TILES) for h in range(IH)]
AFTER_IDX = {6 + n // 2: [n - n % 2, n - n % 2 + 1] for n in range(len(IDX_STEPS))}
AFTER_WS = JOB_VA[2]
LN_TILES = {JOB_ZB[0]: [0, 1], JOB_ZB[1]: [2, 3]}
AFTER_MIX = {JOB_ZB[3]: [0, 1], JOB_ZA[0]: [2, 3]}
ATT_STEPS = [(h, b) for b in range(TILES) for h in range(HEADS)]
_slots = list(range(JOB_ZA[2], JOB_GA[-1] + 1)) + JOB_OA[1::2] + JOB_GB
AFTER_ATT = {_slots[i]: i for i in range(len(ATT_STEPS) + 2)}
SPLIT_YB = {JOB_GB[4]: [0, 1], JOB_GB[5]: [2], JOB_GB[6]: [3]}
assert min(SPLIT_YB) > max(AFTER_ATT)
ROUNDS = TOPK // 8
TOPK_SLOTS = {10: [(1, 1)], 11: [(1, 1)], 12: [(1, 2)], 13: [(1, 2)], 14: [(1, 2)], 15: [(1, 3)], 16: [(1, 3)],
              17: [(1, 2)], 18: [(2, 3)], 19: [(2, 3)], 20: [(2, 3)], 21: [(2, 3)], 22: [(2, 3)],
              23: [(2, 1), (3, 2)], 28: [(3, 2)], 29: [(3, 1)], **{s: [(3, 1)] for s in range(32, 43)}}


class Signal:

    def __init__(self, ctx, nc, name, per_layer, seeded=True):
        self.sem, self.per = ctx.enter_context(nc.semaphore(name)), per_layer
        self.seeded = seeded

    def at(self, layer, n):
        return layer * self.per + (self.per if self.seeded else 0) + n


class Steps:

    def __init__(self, ctx, nc, name):
        self.sem, self.n, self.waited = ctx.enter_context(nc.semaphore(name)), 0, 0

    def link(self, engine, instruction):
        self.mark(instruction)
        self.join(engine)

    def mark(self, instruction):
        self.n += 1
        instruction.then_inc(self.sem, 1)

    def join(self, engine):
        if self.n > self.waited:
            engine.wait_ge(self.sem, self.n)
            self.waited = self.n

    def end_layer(self, engine):
        self.join(engine)
        engine.sem_clear(self.sem)
        self.n = self.waited = 0


def trunk(nc, x, norm_g, w_in, gate_b, a_ln_g, a_ln_b, a_ws, a_bs, q_norm_g, k_norm_g, w_oa, w_ob, w_out,
          ident, rope_cs, out):
    ctx = ExitStack()
    with ctx:
        def sb(name, shape, dt=F32, keep=ctx):
            return keep.enter_context(nc.sbuf_tensor(name, shape, dt))

        w_hi1 = sb("w_hi1", [P, KD, W512], F32R)
        with ExitStack() as early:
            index_hi = sb("index_hi", [P, KD, INDEX], F32R, keep=early)
            s_raw = sb("s_raw", [P, KD, SMALL], keep=early)
        w_hi0 = sb("w_hi0", [P, KD, W512], F32R)
        with ExitStack() as early:
            v_a = sb("v_a", [P, TILES, A_WIDTH], keep=early)
            with ExitStack() as inner:
                u_a = sb("u_a", [P, A_GROUPS, SEQ], keep=inner)
            with ExitStack() as inner:
                qi_t = sb("qi_t", [P, 2, IH // 2, SEQ - P], F32R, keep=inner)
                ki_hi = sb("ki_hi", [P, SEQ], F32R, keep=inner)
                ki_lo = sb("ki_lo", [P, SEQ], F32R, keep=inner)
        g_a = sb("g_a", [P, KD, SEQ])
        with ExitStack() as early:
            x_sb = sb("x_sb", [P, TILES, D], keep=early)
        z_b = sb("z_b", [P, HEADS, SEQ])
        v_b = sb("v_b", [P, TILES, HEADS * DH])
        w_raw = sb("w_raw", [P, RAW, 2, W512])
        h_hi = sb("h_hi", [P, KD, SEQ], F32R)
        h_lo = sb("h_lo", [P, KD, SEQ], F32R)
        w_lo1 = sb("w_lo1", [P, KD, W512], F32R)
        with ExitStack() as early:
            index_lo = sb("index_lo", [P, KD, INDEX], F32R, keep=early)
        w_lo0 = sb("w_lo0", [P, KD, W512], F32R)
        with ExitStack() as early:
            q_t = sb("q_t", [P, HEADS, SEQ], keep=early)
            with ExitStack() as inner:
                k_t = sb("k_t", [P, HEADS, SEQ], keep=inner)
            with ExitStack() as inner:
                xn = sb("xn", [P, 2, D], keep=inner)
        yb_lo = sb("yb_lo", [P, HEADS, SEQ], F32R)
        yb_hi = sb("yb_hi", [P, HEADS, SEQ], F32R)
        with ExitStack() as early:
            norm_bc = sb("norm_bc", [P, D], keep=early)
            lng_bc = sb("lng_bc", [P, A_WIDTH], keep=early)
            lnb_bc = sb("lnb_bc", [P, A_WIDTH], keep=early)
            bs_bc = sb("bs_bc", [P, A_GROUPS, P], keep=early)
            ws_raw = sb("ws_raw", [P, A_GROUPS, P], keep=early)
            ws_t = sb("ws_t", [P, A_GROUPS, P], keep=early)
            kg_bc = sb("kg_bc", [P, DH], keep=early)
            qg_bc = sb("qg_bc", [P, DH], keep=early)
        with ExitStack() as early:
            ya_hi = sb("ya_hi", [P, A_GROUPS, SEQ], F32R, keep=early)
            ya_lo = sb("ya_lo", [P, A_GROUPS, SEQ], F32R, keep=early)
        g_b = sb("g_b", [P, KD, SEQ])
        with ExitStack() as early:
            stage = sb("stage", [P, 2, ROT_I + IH], keep=early)
            rope_a = sb("rope_a", [P, ROT_I], keep=early)
            rope_b = sb("rope_b", [P, ROT_I], keep=early)
        t_half = sb("t_half", [P, 2, SEQ])
        silu_z = sb("silu_z", [P, SEQ])
        um = sb("um", [P, (2 * (ROT_I + IH) + 2 * ROT_I) - 3 * SEQ])
        rot = sb("rot", [P, ROT_I + ID])
        probs = sb("probs", [P, 2, SEQ])
        probs_t = sb("probs_t", [P, SEQ])
        score = sb("score", [P, sum(P * (b + 1) for b in range(1, TILES))])
        eye = sb("eye", [P, P])
        rope = sb("rope", [P, TILES, DH + ID])
        cq, sq, ci, si = (rope[:, :, a:b] for a, b in
                          ((0, DH // 2), (DH // 2, DH), (DH, DH + ID // 2), (DH + ID // 2, DH + ID)))
        diag = sb("diag", [P, P])
        gate_raw = sb("gate_raw", [P, 2 * KD])
        gate_half = sb("gate_half", [P, 2 * KD])
        eps = sb("eps", [P, 1])
        head_w = sb("head_w", [P, TILES, IH])
        top8 = sb("top8", [P, 8])
        ms = sb("ms", [P, 2 * TILES * HEADS + TILES])
        std = sb("std", [P, 2 * TILES * HEADS + TILES])
        rstd = sb("rstd", [P, 2 * TILES * HEADS + TILES])
        bn = sb("bn", [P, TILES, 6])
        mv = sb("mv", [P, TILES, 2])
        ln_std = sb("ln_std", [P, TILES])
        ln_rstd = sb("ln_rstd", [P, TILES])
        row_max = sb("row_max", [P, len(ATT_STEPS)])
        neg_max = sb("neg_max", [P, len(ATT_STEPS)])
        row_sum = sb("row_sum", [P, len(ATT_STEPS)])
        row_inv = sb("row_inv", [P, len(ATT_STEPS)])

        bank = [ctx.enter_context(nc.psum_tensor(f"bank{i}", [P, W512], F32)) for i in range(8)]

        def sig(name, per, seeded=True):
            return Signal(ctx, nc, name, per, seeded)

        s_x0 = [ctx.enter_context(nc.semaphore(f"x_in{t}")) for t in range(TILES)]
        s_small_in = sig("small_weights_in", 16, False)
        s_norm = sig("norm_in", 16, False)
        s_rope = sig("rope_tables_in", 16, False)
        s_kq = sig("k_and_q_gains_in", 32, False)
        s_par = sig("parameters_in", 16 * N_PARAMS, False)
        s_wraw = [sig(f"weights_raw{i}", 16 * len(GROUPS) * NQ // RAW, False) for i in range(RAW)]
        s_whi = sig("weights_hi", len(GROUPS) * NQ)
        s_wlo = sig("weights_lo", len(GROUPS) * NQ)
        s_shi = sig("small_weights_hi", 1)
        s_slo = sig("small_weights_lo", 1)
        s_init = ctx.enter_context(nc.semaphore("tiles_initialised"))
        s_ghalf = sig("gate_bias_halved", 1)
        s_xstd = sig("x_std", TILES)
        s_xn = sig("x_normalised", TILES)
        s_xt = sig("x_transposed", 2 * TILES)
        s_hhi = sig("h_hi_written", 2 * TILES)
        s_hlo = sig("h_lo_written", 2 * TILES)
        s_job = sig("job_done", NJOBS)
        s_free = [sig(f"bank_free{i}", NJOBS // GBANKS) for i in range(GBANKS)]
        s_small = sig("bank7_copied", TILES)
        s_stage = sig("tile_staged", 3 * TILES)
        s_xg = sig("heads_scaled", 2 * TILES)
        s_cos = sig("tile_times_cos", 3 * TILES)
        s_rinv = sig("heads_rstd", 2 * TILES)
        s_rot = sig("tile_rotated", 3 * TILES)
        s_rott = sig("rotated_transposed", 3 * TILES)
        s_rotc = sig("rotated_copied", 3 * TILES)
        s_ilo = sig("index_lo_written", TILES)
        s_idxp = sig("index_logits", len(IDX_STEPS))
        s_relu = sig("index_relu", len(IDX_STEPS))
        s_idx = sig("index_added", len(IDX_STEPS))
        s_va = sig("va_gelu", TILES)
        s_u = sig("u_gelu", TILES)
        s_wst = sig("ws_transposed", 1)
        s_wsc = sig("ws_copied", 1)
        s_wsz = sig("ws_masked", 1)
        s_lnv = sig("ln_variance", 1)
        s_lnstd = sig("ln_std", 1)
        s_ln = sig("ln_applied", TILES)
        s_mix = sig("mixed", A_GROUPS)
        s_um = sig("u_times_mixed", A_GROUPS)
        s_tanh = sig("tanh_half_z", 8)
        s_zused = sig("tanh_half_z_used", 8)
        s_ya = sig("ya_ready", A_GROUPS)
        s_yahi = sig("ya_hi_written", A_GROUPS)
        s_yalo = sig("ya_lo_written", A_GROUPS)
        s_ga = sig("gate_a", KD)
        s_gb = sig("gate_b", KD)
        s_ma = sig("branch_a_gated", KD)
        s_sum = sig("branches_added", KD)
        s_mhi = sig("merged_hi", KD)
        s_mlo = sig("merged_lo", KD)
        s_qk = sig("scores", len(ATT_STEPS))
        s_max = sig("score_max", len(ATT_STEPS))
        s_exp = sig("exponentials", len(ATT_STEPS))
        s_prob = sig("probs_scaled", len(ATT_STEPS))
        s_pt = sig("probs_transposed", len(ATT_STEPS))
        s_ptc = sig("probs_t_copied", len(ATT_STEPS))
        s_pv = sig("attended", len(ATT_STEPS))
        s_yb = sig("yb_ready", TILES)
        s_ybhi = sig("yb_hi_written", HEADS)
        s_yblo = sig("yb_lo_written", HEADS)
        s_xback = sig("x_reloaded", 16, False)
        s_res = sig("residual_added", 2 * TILES)
        s_out = ctx.enter_context(nc.semaphore("out_stored"))
        s_stash = sig("x_stashed_tiles_01", 16, False)
        s_stash2 = sig("x_stashed_tiles_23", 16, False)
        s_eye = ctx.enter_context(nc.semaphore("identity_in"))
        vec = Steps(ctx, nc, "vector_steps")
        act_ = Steps(ctx, nc, "scalar_steps")
        poo = Steps(ctx, nc, "gpsimd_steps")

        def seed(engine, *signals):
            for s in signals:
                engine.sem_inc(s.sem, s.per)

        waits_over = ctx.enter_context(nc.semaphore("waits_over"))

        def pause(engine):
            engine.sem_inc(waits_over, 1)

        block = ctx.enter_context(nc.Block())

        def block_cols(b):
            at = sum(P * (c + 1) for c in range(1, b))
            return slice(at, at + P * (b + 1))

        def weights(g):
            if g == 0:
                return index_hi[:, :, 0:W512], index_lo[:, :, 0:W512]
            return (w_hi1[:], w_lo1[:]) if g % 2 else (w_hi0[:], w_lo0[:])

        def slot_free(layer, g):
            return s_job.at(layer, FIRST_JOB[g - 1] if g >= 2 else FIRST_JOB[g - 1 + len(GROUPS)] - NJOBS)

        def quarters_in(j, engine):
            g = next(i for i in range(len(GROUPS)) if FIRST_JOB[i] <= j < FIRST_JOB[i + 1])
            if g + 1 == len(GROUPS):
                return []
            slots = [0, 1, 2, 2] if GROUPS[g][3] == NQ else dict(scalar=[0, 1, 2, 3], vector=[1, 2, 4, 5])[engine]
            return [(g + 1, qt) for qt in range(NQ) if slots[qt] == j - FIRST_JOB[g]]

        @block.sync
        def _(sp):
            sp.dma_start(x_sb[:, ORDER[0], :], x[ORDER[0] * P:(ORDER[0] + 1) * P, :]).then_inc(s_x0[0], 16)
            with sp.Fori(0, DEPTH) as layer:
                for g, (name, matrix, col, _) in enumerate(GROUPS):
                    src = dict(w_in=w_in, w_oa=w_oa, w_ob=w_ob, w_out=w_out)[matrix][bass.ds(layer, 1)]
                    for qt in range(NQ):
                        n = g * NQ + qt
                        sp.wait_ge(s_wlo.sem, s_wlo.at(layer, n - RAW + 1))
                        pause(sp)
                        if matrix in ("w_oa", "w_ob"):
                            part = src[:, qt * P:(qt + 1) * P, :].rearrange("a p (c n) -> (a p) c n", c=2)
                        else:
                            part = src[:, 2 * qt * P:(2 * qt + 2) * P, col:col + W512] \
                                .rearrange("a (k p) n -> p (a k) n", p=P)
                        sp.dma_start(w_raw[:, n % RAW], part).then_inc(s_wraw[n % RAW].sem, 16)
            for i in range(2 * TILES):
                t, cols = ORDER[i % TILES], slice(i // TILES * W512, (i // TILES + 1) * W512)
                sp.wait_ge(s_res.sem, s_res.at(DEPTH - 1, i + 1))
                sp.dma_start(out[t * P:(t + 1) * P, cols], x_sb[:, t, cols]).then_inc(s_out, 16)
            sp.wait_ge(s_out, 16 * 2 * TILES)

        @block.gpsimd
        def _(pool):
            seed(pool, s_xg, s_cos)

            def norm_in(l):
                pool.dma_start(norm_bc[:], norm_g[l].to_broadcast([P, D])).then_inc(s_norm.sem, 16)

            norm_in(slice(0, 1))
            with pool.Fori(0, DEPTH) as layer:
                l = bass.ds(layer, 1)
                pool.wait_ge(s_mlo.sem, s_mlo.at(layer, 0))
                pause(pool)
                pool.dma_start(s_raw[:], w_in[l, :, COL["ik"]:COL["ik"] + SMALL]
                               .rearrange("a (k p) n -> p (a k) n", p=P)).then_inc(s_small_in.sem, 16)
                pool.wait_ge(s_xn.sem, s_xn.at(layer, 1))
                pause(pool)
                pool.dma_start(rope[:], rope_cs).then_inc(s_rope.sem, 16)
                for dst, src in ((kg_bc, k_norm_g), (qg_bc, q_norm_g)):
                    pool.dma_start(dst[:], src[l].to_broadcast([P, dst.shape[1]])).then_inc(s_kq.sem, 16)
                parameters = [
                    (lng_bc, a_ln_g[l].to_broadcast([P, A_WIDTH])),
                    (lnb_bc, a_ln_b[l].to_broadcast([P, A_WIDTH])),
                    (bs_bc, a_bs[l].rearrange("a (g i) -> a g i", g=A_GROUPS).to_broadcast([P, A_GROUPS, P])),
                    (ws_raw, a_ws[l].rearrange("a g i j -> i (a g) j")),
                    (gate_raw, gate_b[l].rearrange("a p c -> (a p) c"))]
                pool.wait_ge(s_xn.sem, s_xn.at(layer, 2))
                pool.wait_ge(s_res.sem, s_res.at(layer, 0))
                for t in range(TILES):
                    pool.wait_ge(s_x0[t], 16)
                pause(pool)
                stash = out.rearrange("(t p) d -> p t d", p=P)
                pool.dma_start(stash[:, 0:2], x_sb[:, 0:2]).then_inc(s_stash.sem, 16)
                pool.wait_ge(s_kq.sem, s_kq.at(layer, 32))
                pool.wait_ge(s_rope.sem, s_rope.at(layer, 16))

                def times_cos(n, tile, heads, dim, cos):
                    pool.wait_ge(s_rot.sem, s_rot.at(layer, n))
                    nc.gpsimd.tensor_tensor(
                        rope_a[:, 0:heads * dim].rearrange("p (h d) -> p h d", h=2 * heads),
                        tile.rearrange("p (h d) -> p h d", h=2 * heads),
                        cos.unsqueeze(1).to_broadcast([P, 2 * heads, dim // 2]), ALU.mult).then_inc(s_cos.sem, 1)

                for n in range(TILES):
                    pool.wait_ge(s_stage.sem, s_stage.at(layer, n + 1))
                    b = ORDER[n]
                    first = 0 if b else IH
                    times_cos(n, stage[:, n % 2, first * ID:ROT_I], IH + 1 - first, ID, ci[:, b])
                for n in range(2 * TILES):
                    g_bc = kg_bc if n < TILES else qg_bc
                    tile = stage[:, (TILES + n) % 2, 0:HEADS * DH].rearrange("p (h d) -> p h d", h=HEADS)
                    pool.wait_ge(s_rinv.sem, s_rinv.at(layer, n + 1))
                    poo.link(pool, nc.gpsimd.tensor_tensor(
                        tile, tile, rstd[:, HEADS * n:HEADS * n + HEADS].unsqueeze(2).to_broadcast([P, HEADS, DH]),
                        ALU.mult))
                    nc.gpsimd.tensor_tensor(tile, tile, g_bc[:].unsqueeze(1).to_broadcast([P, HEADS, DH]),
                                            ALU.mult).then_inc(s_xg.sem, 1)
                    pool.wait_ge(s_xg.sem, s_xg.at(layer, n + 1))
                    times_cos(TILES + n, stage[:, (TILES + n) % 2, 0:HEADS * DH], HEADS, DH, cq[:, n % TILES])
                    if n == 0:
                        pool.dma_start(stash[:, 2:4], x_sb[:, 2:4]).then_inc(s_stash2.sem, 16)
                    if n < N_PARAMS:
                        dst, src = parameters[n]
                        pool.dma_start(dst[:], src).then_inc(s_par.sem, 16)
                pool.wait_ge(s_yblo.sem, s_yblo.at(layer, HEADS))
                pool.wait_ge(s_stash.sem, s_stash.at(layer, 16))
                pool.wait_ge(s_stash2.sem, s_stash2.at(layer, 16))
                pause(pool)
                pool.dma_start(x_sb[:], out.rearrange("(t p) d -> p t d", p=P)).then_inc(s_xback.sem, 16)
                pool.wait_ge(s_mlo.sem, s_mlo.at(layer + 1, 0))
                pause(pool)
                norm_in(bass.ds(layer + 1, 1))
                pause(pool)
                poo.end_layer(pool)

        @block.tensor
        def _(pe):
            seed(pe, s_job, s_xt, s_rott, s_idxp, s_wst, s_mix, s_qk, s_pt, s_pv)
            pe.wait_ge(s_eye, 16)

            def transpose_x(layer, t):
                pe.wait_ge(s_xn.sem, s_xn.at(layer, t + 1))
                if t >= 2:
                    pe.wait_ge(s_hlo.sem, s_hlo.at(layer, 2 * (t - 1)))
                for half in range(2):
                    dst = bank[3 + 2 * (t % 2) + half]
                    for k in range(4):
                        kk = 4 * half + k
                        last = nc.tensor.transpose(dst[:, k * P:(k + 1) * P], xn[:, t % 2, kk * P:(kk + 1) * P], eye[:])
                    last.then_inc(s_xt.sem, 1)

            def transpose_rotated(layer, n):
                pe.wait_ge(s_rot.sem, s_rot.at(layer, n + 1))
                if n == 0:
                    pe.wait_ge(s_hlo.sem, s_hlo.at(layer, 2 * TILES))
                else:
                    pe.wait_ge(s_rotc.sem, s_rotc.at(layer, n))
                if 1 <= n <= TILES:
                    pe.wait_ge(s_ilo.sem, s_ilo.at(layer, n))
                index = n < TILES
                for c in range(0 if index and ORDER[n] == 0 else 4):
                    last = nc.tensor.transpose(bank[5][:, c * P:(c + 1) * P], rot[:, c * P:(c + 1) * P], eye[:])
                if index:
                    last = nc.tensor.transpose(bank[6][:, 0:P], rot[:, IH * ID:IH * ID + 2 * ID], eye[:])
                last.then_inc(s_rott.sem, 1)

            def index_logits(layer, n):
                b, h = IDX_STEPS[n]
                if n < 2:
                    pe.wait_ge(s_ilo.sem, s_ilo.at(layer, TILES))
                else:
                    pe.wait_ge(s_relu.sem, s_relu.at(layer, n - 1))
                dst, q = bank[3 + n % 2][:, 0:P * (b + 1)], qi_t[:, h % 2, h // 2, (b - 1) * P:b * P]
                nc.tensor.matmul(dst, q, ki_lo[:, 0:P * (b + 1)], start=True, stop=False)
                nc.tensor.matmul(dst, q, ki_hi[:, 0:P * (b + 1)], start=False, stop=True).then_inc(s_idxp.sem, 1)

            def transpose_ws(layer):
                pe.wait_ge(s_par.sem, s_par.at(layer, 16 * N_PARAMS))
                pe.wait_ge(s_rotc.sem, s_rotc.at(layer, 3 * TILES))
                for g in range(A_GROUPS):
                    last = nc.tensor.transpose(bank[5][:, g * P:(g + 1) * P], ws_raw[:, g], eye[:])
                last.then_inc(s_wst.sem, 1)

            def mix(layer, g):
                if g == 0:
                    pe.wait_ge(s_ln.sem, s_ln.at(layer, TILES))
                    pe.wait_ge(s_wsc.sem, s_wsc.at(layer, 1))
                    pe.wait_ge(s_wsz.sem, s_wsz.at(layer, 1))
                    pe.wait_ge(s_relu.sem, s_relu.at(layer, len(IDX_STEPS)))
                for n in range(TILES):
                    last = nc.tensor.matmul(bank[3 + g][:, n * P:(n + 1) * P], v_a[:, n, g * P:(g + 1) * P],
                                            ws_t[:, g], start=True, stop=True)
                last.then_inc(s_mix.sem, 1)

            def attend(layer, i):
                if i >= 2:
                    h, b = ATT_STEPS[i - 2]
                    pe.wait_ge(s_ptc.sem, s_ptc.at(layer, i - 1))
                    if h == 0 and b:
                        pe.wait_ge(s_yb.sem, s_yb.at(layer, b))
                    for c in range(b + 1):
                        last = nc.tensor.matmul(bank[7][:, h * P:(h + 1) * P], v_b[:, c, h * DH:(h + 1) * DH],
                                                probs_t[:, c * P:(c + 1) * P], start=(c == 0), stop=(c == b))
                    last.then_inc(s_pv.sem, 1)
                if 1 <= i <= len(ATT_STEPS):
                    h, b = ATT_STEPS[i - 1]
                    pe.wait_ge(s_prob.sem, s_prob.at(layer, i))
                    if i >= 2:
                        pe.wait_ge(s_ptc.sem, s_ptc.at(layer, i - 1))
                    for c in range(b + 1):
                        last = nc.tensor.transpose(bank[5][:, c * P:(c + 1) * P],
                                                   probs[:, (i - 1) % 2, c * P:(c + 1) * P], eye[:])
                    last.then_inc(s_pt.sem, 1)
                if i < len(ATT_STEPS):
                    h, b = ATT_STEPS[i]
                    if i == 0:
                        pe.wait_ge(s_um.sem, s_um.at(layer, A_GROUPS))
                    if i >= 2:
                        pe.wait_ge(s_max.sem, s_max.at(layer, i - 1))
                    nc.tensor.matmul(bank[3 + i % 2][:, 0:P * (b + 1)], q_t[:, h, b * P:(b + 1) * P],
                                     k_t[:, h, 0:P * (b + 1)], start=True, stop=True).then_inc(s_qk.sem, 1)

            def three_pass(dst, pairs, ready=None):
                for n, (s_h, s_l, m_h, m_l) in enumerate(pairs):
                    if ready:
                        ready(n)
                    nc.tensor.matmul(dst, s_h, m_l, start=(n == 0), stop=False)
                    nc.tensor.matmul(dst, s_l, m_h, start=False, stop=False)
                    last = nc.tensor.matmul(dst, s_h, m_h, start=False, stop=(n == len(pairs) - 1))
                return last

            def job(layer, g, j):
                name = GROUPS[g][0]
                n = FIRST_JOB[g] + j
                w_hi, w_lo = weights(g)
                dst = bank[n % GBANKS]
                pe.wait_ge(s_free[n % GBANKS].sem, s_free[n % GBANKS].at(layer, n // GBANKS))
                if name in ("oa", "ob"):
                    y_hi, y_lo = (ya_hi, ya_lo) if name == "oa" else (yb_hi, yb_lo)
                    done = s_yalo if name == "oa" else s_yblo
                    pairs = []
                    for k in range(A_GROUPS):
                        c = slice((j % 4) * P, (j % 4 + 1) * P)
                        piece = 2 * k + j // 4
                        pairs.append((w_hi[:, piece, c], w_lo[:, piece, c], y_hi[:, k], y_lo[:, k]))

                    def ready(k):
                        if j == 0:
                            pe.wait_ge(s_wlo.sem, s_wlo.at(layer, NQ * g + k + 1))
                            pe.wait_ge(done.sem, done.at(layer, k + 1))
                else:
                    t = ORDER[j] if name == "out" else j
                    tok = slice(t * P, (t + 1) * P)
                    if name in TOKEN_MAJOR:
                        pairs = [(h_hi[:, k, tok], h_lo[:, k, tok], w_hi[:, k], w_lo[:, k])
                                 for k in range(KD)]
                    else:
                        pairs = [(w_hi[:, k, tok], w_lo[:, k, tok], h_hi[:, k], h_lo[:, k])
                                 for k in range(KD)]
                    def ready(k):
                        if j == 0 and k % 2 == 0:
                            pe.wait_ge(s_wlo.sem, s_wlo.at(layer, NQ * g + k // 2 + 1))
                        if name == "out" and n == JOB_OUT[0]:
                            pe.wait_ge(s_mlo.sem, s_mlo.at(layer, k + 1))
                last = three_pass(dst[:], pairs, ready)
                last.then_inc(s_job.sem, 1)

            def index_job(layer, t):
                tok, half = slice(ORDER[t] * P, (ORDER[t] + 1) * P), INDEX // 2
                pe.wait_ge(s_free[t % GBANKS].sem, s_free[t % GBANKS].at(layer, t // GBANKS))

                def products(dst, first, k, width=half):
                    for n, (h, w) in enumerate(((h_hi, index_lo), (h_lo, index_hi), (h_hi, index_hi))):
                        last = nc.tensor.matmul(dst[:, 0:width], h[:, k, tok], w[:, k, first:first + width],
                                                start=(k == 0 and n == 0), stop=(k == KD - 1 and n == 2))
                    return last

                if ORDER[t] == 0:
                    for k in range(KD):
                        if k % (KD // 2) == 0:
                            pe.wait_ge(s_hlo.sem, s_hlo.at(layer, 2 * t + k // (KD // 2) + 1))
                        last = products(bank[t % GBANKS], IH * ID, k, SMALL)
                    last.then_inc(s_job.sem, 1)
                    return
                for ks in ((range(KD // 2), range(KD // 2, KD)) if t == 0 else (range(KD),)):
                    for k in ks:
                        if k % (KD // 2) == 0:
                            pe.wait_ge(s_hlo.sem, s_hlo.at(layer, 2 * t + k // (KD // 2) + 1))
                        if k == KD // 2 and t + 1 < TILES:
                            transpose_x(layer, t + 1)
                        if t == 0 and k % 2 == 0:
                            pe.wait_ge(s_wlo.sem, s_wlo.at(layer, k // 2 + 1))
                        products(bank[t % GBANKS], 0, k)
                    if t == 0:
                        pe.wait_ge(s_slo.sem, s_slo.at(layer, 1))
                    pe.wait_ge(s_small.sem, s_small.at(layer, t))
                    for k in ks:
                        if t == 2 and k == KD // 2:
                            transpose_rotated(layer, 0)
                        last = products(bank[7], half, k)
                last.then_inc(s_job.sem, 1)

            for _ in range(WARM_UP):
                nc.tensor.transpose(bank[6][:, 0:P], eye[:], eye[:])
            with pe.Fori(0, DEPTH) as layer:
                transpose_x(layer, 0)
                for g in range(len(GROUPS)):
                    for j in range(GROUPS[g][3]):
                        n = FIRST_JOB[g] + j
                        if g == 0:
                            index_job(layer, j)
                        else:
                            job(layer, g, j)
                        if AFTER_QI.get(n, 0):
                            transpose_rotated(layer, AFTER_QI[n])
                        if n in AFTER_K:
                            transpose_rotated(layer, TILES + AFTER_K[n])
                        if n in AFTER_Q:
                            transpose_rotated(layer, 2 * TILES + AFTER_Q[n])
                        for step in AFTER_IDX.get(n, []):
                            index_logits(layer, step)
                        if n == AFTER_WS:
                            transpose_ws(layer)
                        for group in AFTER_MIX.get(n, []):
                            mix(layer, group)
                        if n in AFTER_ATT:
                            attend(layer, AFTER_ATT[n])

        @block.scalar
        def _(act):
            seed(act, s_whi, s_shi, s_xstd, s_hhi, s_small, s_stage, s_rotc, s_relu, s_va, s_u, s_wsc,
                 s_lnstd, s_tanh, s_yahi, s_ga, s_gb, s_mhi, s_exp, s_ptc, s_ybhi, *s_free)

            act.dma_start(eye[:], ident).then_inc(s_eye, 16)
            for i, t in enumerate(ORDER[1:]):
                act.dma_start(x_sb[:, t, :], x[t * P:(t + 1) * P, :]).then_inc(s_x0[i + 1], 16)

            def rounded(layer, g, qt):
                n = g * NQ + qt
                act.wait_ge(s_wraw[n % RAW].sem, s_wraw[n % RAW].at(layer, 16 * (n // RAW + 1)))
                act.wait_ge(s_job.sem, slot_free(layer, g))
                nc.scalar.activation(weights(g)[0][:, 2 * qt:2 * qt + 2], w_raw[:, n % RAW], ACT.Copy) \
                    .then_inc(s_whi.sem, 1)

            def root(layer, dst, src, scale=1.0):
                return nc.scalar.activation(dst, src, ACT.Sqrt, bias=eps[:], scale=scale)

            def head_std(layer, n, src):
                c = HEADS * n
                for h in range(HEADS):
                    act_.mark(nc.scalar.activation(bank[7][:, h * DH:(h + 1) * DH], src[:, h * DH:(h + 1) * DH], ACT.Square,
                                                   scale=DH ** -0.5, accum_out=ms[:, c + h:c + h + 1]))
                act_.join(act)
                act_.mark(root(layer, std[:, c:c + HEADS], ms[:, c:c + HEADS]))

            def evacuate(layer, n):
                src, free = bank[n % GBANKS], s_free[n % GBANKS]
                if n in JOB_OA + JOB_OB + JOB_OUT:
                    return
                act.wait_ge(s_job.sem, s_job.at(layer, n + 1))
                if n in JOB_IQ:
                    t = n - JOB_IQ[0]
                    act.wait_ge(s_rot.sem, s_rot.at(layer, t - 1))
                    if t == 0:
                        act.wait_ge(s_zused.sem, s_zused.at(layer, 0))
                    if ORDER[t] == 0:
                        act_.mark(nc.scalar.activation(stage[:, t % 2, IH * ID:INDEX], src[:, 0:SMALL], ACT.Copy))
                    else:
                        half = INDEX // 2
                        act_.mark(nc.scalar.activation(stage[:, t % 2, half:INDEX], bank[7][:, 0:half], ACT.Copy))
                        act_.mark(nc.scalar.activation(stage[:, t % 2, 0:half], src[:, 0:half], ACT.Copy))
                    act_.join(act)
                    act.sem_inc(free.sem, 1)
                    act.sem_inc(s_small.sem, 1)
                    act.sem_inc(s_stage.sem, 1)
                elif n in JOB_K or n in JOB_Q:
                    t = n - JOB_K[0]
                    act.wait_ge(s_rot.sem, s_rot.at(layer, TILES + t - 1))
                    head_std(layer, t, src)
                    act_.mark(nc.scalar.activation(stage[:, (TILES + t) % 2, 0:HEADS * DH], src[:], ACT.Copy))
                    act_.join(act)
                    act.sem_inc(free.sem, 1)
                    act.sem_inc(s_stage.sem, 1)
                elif n in JOB_VB:
                    t = n - JOB_VB[0]
                    if t == 0:
                        act.wait_ge(s_stash2.sem, s_stash2.at(layer, 16))
                    act_.mark(nc.scalar.activation(v_b[:, t], src[:], ACT.Copy))
                    act_.join(act)
                    act.sem_inc(free.sem, 1)
                elif n in JOB_VA or n in JOB_U:
                    dst, done, t = (v_a, s_va, n - JOB_VA[0]) if n in JOB_VA else (u_a, s_u, n - JOB_U[0])
                    act_.mark(nc.scalar.activation(dst[:, t], src[:], ACT.Gelu_apprx_tanh))
                    act_.join(act)
                    act.sem_inc(free.sem, 1)
                    act.sem_inc(done.sem, 1)
                elif n in JOB_ZB or n in JOB_ZA:
                    t = n - JOB_ZB[0]
                    if n == JOB_ZB[0]:
                        act.wait_ge(s_lnv.sem, s_lnv.at(layer, 1))
                        root(layer, ln_std[:], mv[:, :, 1]).then_inc(s_lnstd.sem, 1)
                    act.wait_ge(s_zused.sem, s_zused.at(layer, t - 1))
                    if t == 0:
                        act.wait_ge(s_rot.sem, s_rot.at(layer, 3 * TILES))
                    nc.scalar.activation(t_half[:, t % 2], src[:], ACT.Tanh, scale=0.5).then_inc(s_tanh.sem, 1)
                elif n in JOB_GA or n in JOB_GB:
                    dst, done, d, c = (g_a, s_ga, n - JOB_GA[0], 0) if n in JOB_GA else (g_b, s_gb, n - JOB_GB[0], KD)
                    if n == JOB_GA[0]:
                        act.wait_ge(s_mix.sem, s_mix.at(layer, A_GROUPS))
                        act.wait_ge(s_ghalf.sem, s_ghalf.at(layer, 1))
                    if n == JOB_GA[4]:
                        act.wait_ge(s_yalo.sem, s_yalo.at(layer, A_GROUPS))
                    if n == JOB_GB[0]:
                        act.wait_ge(s_job.sem, s_job.at(layer, JOB_OA[-1] + 1))
                    act_.mark(nc.scalar.activation(dst[:, d], src[:], ACT.Tanh, scale=0.5,
                                                   bias=gate_half[:, c + d:c + d + 1]))
                    act_.join(act)
                    act.sem_inc(free.sem, 1)
                    act.sem_inc(done.sem, 1)

            def rotated_copied(layer, n):
                for after, base in ((AFTER_QI, 0), (AFTER_K, TILES), (AFTER_Q, 2 * TILES)):
                    if n in after:
                        t = after[n]
                        act.wait_ge(s_rott.sem, s_rott.at(layer, base + t + 1))
                        four = bank[5][:].rearrange("p (c q) -> p c q", c=4)
                        if base == 0:
                            if t == 0:
                                act.wait_ge(s_stash.sem, s_stash.at(layer, 16))
                                act.wait_ge(s_xt.sem, s_xt.at(layer, 2 * TILES))
                            b = ORDER[t]
                            for odd in range(2 if b else 0):
                                part = slice(ID * odd, ID * odd + ID)
                                act_.mark(nc.scalar.activation(qi_t[part, odd, :, (b - 1) * P:b * P], four[part],
                                                               ACT.Copy))
                            act_.mark(nc.scalar.activation(ki_hi[:, b * P:(b + 1) * P], bank[6][:, 0:P], ACT.Copy))
                        else:
                            dst = k_t if base == TILES else q_t
                            act_.mark(nc.scalar.activation(dst[:, :, t * P:(t + 1) * P], four, ACT.Copy))
                        act_.join(act)
                        act.sem_inc(s_rotc.sem, 1)

            def beside(layer, n):
                for i in AFTER_IDX.get(n, []):
                    b, h = IDX_STEPS[i]
                    w = P * (b + 1)
                    act.wait_ge(s_idxp.sem, s_idxp.at(layer, i + 1))
                    if i >= 2:
                        act.wait_ge(s_idx.sem, s_idx.at(layer, i - 1))
                    nc.scalar.activation(probs[:, i % 2, 0:w], bank[3 + i % 2][:, 0:w], ACT.Relu).then_inc(s_relu.sem, 1)
                if n == AFTER_WS:
                    act.wait_ge(s_wst.sem, s_wst.at(layer, 1))
                    four = bank[5][:].rearrange("p (c q) -> p c q", c=A_GROUPS)
                    act_.mark(nc.scalar.activation(ws_t[0:CHUNK], four[0:CHUNK], ACT.Copy))
                    act_.mark(nc.scalar.activation(ws_t[CHUNK:P, :, CHUNK:P], four[CHUNK:P, :, CHUNK:P], ACT.Copy))
                    act_.join(act)
                    act.sem_inc(s_wsc.sem, 1)
                if n - 1 in JOB_ZA:
                    c = n - 1 - JOB_ZA[0]
                    act.wait_ge(s_ya.sem, s_ya.at(layer, c + 1))
                    nc.scalar.activation(ya_hi[:, c], u_a[:, c], ACT.Copy).then_inc(s_yahi.sem, 1)
                if n in AFTER_ATT:
                    i = AFTER_ATT[n]
                    if i >= 1 and i <= len(ATT_STEPS):
                        b = ATT_STEPS[i - 1][1]
                        w = P * (b + 1)
                        act.wait_ge(s_pt.sem, s_pt.at(layer, i))
                        if i >= 2:
                            act.wait_ge(s_pv.sem, s_pv.at(layer, i - 1))
                        nc.scalar.activation(probs_t[:, 0:w], bank[5][:, 0:w], ACT.Copy).then_inc(s_ptc.sem, 1)
                    if i < len(ATT_STEPS):
                        w = P * (ATT_STEPS[i][1] + 1)
                        act.wait_ge(s_max.sem, s_max.at(layer, i + 1))
                        act_.mark(nc.scalar.activation(probs[:, i % 2, 0:w], probs[:, i % 2, 0:w], ACT.Exp,
                                                       bias=neg_max[:, i:i + 1], scale=ATT_SCALE,
                                                       accum_out=row_sum[:, i:i + 1]))
                        act_.join(act)
                        act.sem_inc(s_exp.sem, 1)
                for h in SPLIT_YB.get(n, []):
                    act.wait_ge(s_yb.sem, s_yb.at(layer, TILES))
                    nc.scalar.activation(yb_hi[:, h], z_b[:, h], ACT.Copy).then_inc(s_ybhi.sem, 1)
                if n in JOB_OB:
                    d = n - JOB_OB[0]
                    act.wait_ge(s_sum.sem, s_sum.at(layer, d + 1))
                    if d == 0:
                        act.wait_ge(s_job.sem, s_job.at(layer, JOB_GB[-1] + 1))
                    nc.scalar.activation(h_hi[:, d], g_b[:, d], ACT.Copy, scale=0.5).then_inc(s_mhi.sem, 1)

            def x_std(layer, t):
                c = 2 * TILES * HEADS + t
                act.wait_ge(s_res.sem, s_res.at(layer, t + 1 - TILES))
                act.wait_ge(s_x0[t], 16)
                if t == 0:
                    act.wait_ge(s_max.sem, s_max.at(layer, 0))
                act_.link(act, nc.scalar.activation(score[:, 0:D], x_sb[:, ORDER[t]], ACT.Square, scale=D ** -0.5,
                                                    accum_out=ms[:, c:c + 1]))
                root(layer, std[:, c:c + 1], ms[:, c:c + 1]).then_inc(s_xstd.sem, 1)

            def h_rounded(layer, t):
                act.wait_ge(s_job.sem, s_job.at(layer, JOB_OUT[TILES + t] + 1 - NJOBS))
                for half in range(2):
                    act.wait_ge(s_xt.sem, s_xt.at(layer, 2 * t + half + 1))
                    nc.scalar.activation(h_hi[:, 4 * half:4 * half + 4, ORDER[t] * P:(ORDER[t] + 1) * P],
                                         bank[3 + 2 * (t % 2) + half][:].rearrange("p (c q) -> p c q", c=4),
                                         ACT.Copy).then_inc(s_hhi.sem, 1)

            def first_tile(layer):
                nc.scalar.preload_act_table(ACT.Sqrt)
                x_std(layer, 0)

            act.wait_ge(s_init, 1)
            first_tile(0)
            act_.end_layer(act)
            with act.Fori(0, DEPTH) as layer:
                rounded(layer, 0, 0)
                rounded(layer, 0, 1)
                h_rounded(layer, 0)
                x_std(layer, 1)
                act.wait_ge(s_small_in.sem, s_small_in.at(layer, 16))
                nc.scalar.activation(index_hi[:, :, W512:INDEX], s_raw[:], ACT.Copy).then_inc(s_shi.sem, 1)
                rounded(layer, 0, 2)
                x_std(layer, 2)
                rounded(layer, 0, 3)
                x_std(layer, 3)
                for n in range(NJOBS):
                    if n + 1 < TILES:
                        h_rounded(layer, n + 1)
                    for g, qt in quarters_in(n, "scalar"):
                        rounded(layer, g, qt)
                    if AFTER_QI.get(n) == 0:
                        rotated_copied(layer, n)
                    evacuate(layer, n)
                    if AFTER_QI.get(n) != 0:
                        rotated_copied(layer, n)
                    beside(layer, n)
                    if n == JOB_OUT[5]:
                        first_tile(layer + 1)
                pause(act)
                act_.end_layer(act)

        @block.vector
        def _(dve):
            seed(dve, s_wlo, s_slo, s_ilo, s_ghalf, s_xn, s_hlo, s_rinv, s_rot, s_idx, s_wsz, s_lnv, s_ln, s_um, s_zused,
                 s_ya, s_yalo, s_ma, s_sum, s_mlo, s_max, s_prob, s_yb, s_yblo, s_res)
            vec.mark(nc.vector.memset(diag[:], 0.0))
            vec.join(dve)
            vec.mark(nc.vector.memset(diag[0:CHUNK, CHUNK:P], FILL))
            vec.mark(nc.vector.memset(eps[:], EPS))
            vec.join(dve)
            dve.sem_inc(s_init, 1)
            vec.end_layer(dve)

            def remainder(layer, g, qt):
                n = g * NQ + qt
                dve.wait_ge(s_whi.sem, s_whi.at(layer, n + 1))
                hi, lo = (w[:, 2 * qt:2 * qt + 2] for w in weights(g))
                nc.vector.tensor_tensor(lo, w_raw[:, n % RAW], hi.bitcast(F32), ALU.subtract) \
                    .then_inc(s_wlo.sem, 1)

            def rotate(layer, n, dst, tile, heads, dim, sin):
                w, half = heads * dim, dim // 2
                src = tile[:, 0:w].rearrange("p (h d) -> p h d", h=heads)
                b = rope_b[:, 0:w].rearrange("p (h d) -> p h d", h=heads)
                first, second, sine = slice(0, half), slice(half, dim), sin.unsqueeze(1).to_broadcast([P, heads, half])
                vec.mark(nc.vector.scalar_tensor_tensor(b[:, :, first], src[:, :, second], -1.0, sine, ALU.mult, ALU.mult))
                vec.mark(nc.vector.tensor_tensor(b[:, :, second], src[:, :, first], sine, ALU.mult))
                vec.join(dve)
                dve.wait_ge(s_cos.sem, s_cos.at(layer, n + 1))
                return nc.vector.tensor_tensor(dst, rope_a[:, 0:w], rope_b[:, 0:w], ALU.add)

            def rotated(layer, n):
                dve.wait_ge(s_rott.sem, s_rott.at(layer, n))
                if n < TILES:
                    if n == 0:
                        dve.wait_ge(s_rope.sem, s_rope.at(layer, 16))
                    dve.wait_ge(s_stage.sem, s_stage.at(layer, n + 1))
                    tile = stage[:, n % 2]
                    b = ORDER[n]
                    vec.mark(nc.vector.tensor_scalar(head_w[:, b], tile[:, ROT_I:ROT_I + IH], IDX_SCALE, None, ALU.mult))
                    first = 0 if b else IH
                    vec.mark(rotate(layer, n, rot[:, first * ID:ROT_I], tile[:, first * ID:ROT_I], IH + 1 - first, ID,
                                    si[:, b]))
                    vec.join(dve)
                    nc.vector.tensor_copy(rot[:, ROT_I:ROT_I + ID], rot[:, IH * ID:ROT_I]).then_inc(s_rot.sem, 1)
                else:
                    m = n - TILES
                    dve.wait_ge(s_xg.sem, s_xg.at(layer, m + 1))
                    rotate(layer, n, rot[:, 0:HEADS * DH], stage[:, n % 2], HEADS, DH, sq[:, m % TILES]).then_inc(s_rot.sem, 1)

            def index_remainder(layer, t):
                dve.wait_ge(s_rotc.sem, s_rotc.at(layer, t + 1))
                b = ORDER[t]
                four, col = bank[5][:].rearrange("p (c q) -> p c q", c=4), slice((b - 1) * P, b * P)
                for odd in range(2 if b else 0):
                    part, other = (slice(ID * o, ID * o + ID) for o in (odd, 1 - odd))
                    vec.mark(nc.vector.tensor_tensor(qi_t[other, odd, :, col], four[part],
                                                     qi_t[part, odd, :, col].bitcast(F32), ALU.subtract))
                col = slice(b * P, (b + 1) * P)
                vec.link(dve, nc.vector.tensor_tensor(ki_lo[:, col], bank[6][:, 0:P], ki_hi[:, col].bitcast(F32),
                                                      ALU.subtract))
                dve.sem_inc(s_ilo.sem, 1)

            def index_add(layer, i):
                b, h = IDX_STEPS[i]
                cols, w = block_cols(b), P * (b + 1)
                weight = head_w[:, b, h:h + 1]
                dve.wait_ge(s_relu.sem, s_relu.at(layer, i + 1))
                if h == 0:
                    op = nc.vector.tensor_scalar(score[:, cols], probs[:, i % 2, 0:w], weight, None, ALU.mult)
                else:
                    op = nc.vector.scalar_tensor_tensor(score[:, cols], probs[:, i % 2, 0:w], weight, score[:, cols],
                                                        ALU.mult, ALU.add)
                op.then_inc(s_idx.sem, 1)
                dve.wait_ge(s_idx.sem, s_idx.at(layer, i + 1))
                if h == IH - 1:
                    last = score[:, cols.stop - P:cols.stop]
                    vec.link(dve, nc.vector.tensor_tensor(last, last, diag[:], ALU.add))

            def topk_round(b, r):
                s = score[:, block_cols(b)]
                vec.link(dve, nc.vector.max(top8[:], s))
                vec.link(dve, nc.vector.match_replace(s, top8[:], s, TAKEN))
                if r == ROUNDS - 1:
                    vec.link(dve, nc.vector.tensor_scalar(s, s, TAKEN, FILL, ALU.not_equal, ALU.mult))

            def attention_scale(layer, i):
                w = P * (ATT_STEPS[i][1] + 1)
                dve.wait_ge(s_exp.sem, s_exp.at(layer, i + 1))
                vec.link(dve, nc.vector.reciprocal(row_inv[:, i:i + 1], row_sum[:, i:i + 1]))
                nc.vector.tensor_scalar(probs[:, i % 2, 0:w], probs[:, i % 2, 0:w], row_inv[:, i:i + 1], None,
                                        ALU.mult).then_inc(s_prob.sem, 1)

            def attention_max(layer, i):
                b = ATT_STEPS[i][1]
                w = P * (b + 1)
                mask = score[:, block_cols(b)] if b else diag[:]
                dve.wait_ge(s_qk.sem, s_qk.at(layer, i + 1))
                if i >= 2:
                    dve.wait_ge(s_pt.sem, s_pt.at(layer, i - 1))
                pause(dve)
                vec.link(dve, nc.vector.tensor_tensor_reduce(
                    out=probs[:, i % 2, 0:w], in0=bank[3 + i % 2][:, 0:w], in1=mask, scale=1.0, scalar=2 * FILL,
                    op0=ALU.add, op1=ALU.max, accum_out=row_max[:, i:i + 1]))
                nc.vector.tensor_scalar(neg_max[:, i:i + 1], row_max[:, i:i + 1], -ATT_SCALE, None,
                                        ALU.mult).then_inc(s_max.sem, 1)

            def merged_lo(layer, d):
                dve.wait_ge(s_mhi.sem, s_mhi.at(layer, d + 1))
                nc.vector.scalar_tensor_tensor(h_lo[:, d], g_b[:, d], 0.5, h_hi[:, d].bitcast(F32),
                                               ALU.mult, ALU.subtract).then_inc(s_mlo.sem, 1)

            def evacuate(layer, n):
                src, free = bank[n % GBANKS], s_free[n % GBANKS]
                if n in JOB_K or n in JOB_Q:
                    m = n - JOB_K[0]
                    c = HEADS * m
                    dve.wait_ge(s_stage.sem, s_stage.at(layer, TILES + m + 1))
                    nc.vector.reciprocal(rstd[:, c:c + HEADS], std[:, c:c + HEADS]).then_inc(s_rinv.sem, 1)
                elif n in JOB_VA:
                    t = n - JOB_VA[0]
                    dve.wait_ge(s_va.sem, s_va.at(layer, t + 1))
                    vec.link(dve, nc.vector.bn_stats(bn[:, t], v_a[:, t]))
                    op = nc.vector.bn_aggr(mv[:, t], bn[:, t])
                    if t < TILES - 1:
                        vec.mark(op)
                    else:
                        vec.link(dve, op)
                        dve.sem_inc(s_lnv.sem, 1)
                elif n in JOB_ZB:
                    c = n - JOB_ZB[0]
                    dve.wait_ge(s_tanh.sem, s_tanh.at(layer, c + 1))
                    if c == 0:
                        dve.wait_ge(s_idxp.sem, s_idxp.at(layer, len(IDX_STEPS)))
                    vec.link(dve, nc.vector.scalar_tensor_tensor(z_b[:, c], t_half[:, c % 2], 1.0, src[:],
                                                                 ALU.add, ALU.mult))
                    dve.sem_inc(free.sem, 1)
                    dve.sem_inc(s_zused.sem, 1)
                elif n in JOB_ZA:
                    c = n - JOB_ZA[0]
                    dve.wait_ge(s_tanh.sem, s_tanh.at(layer, 4 + c + 1))
                    vec.link(dve, nc.vector.scalar_tensor_tensor(silu_z[:], t_half[:, c % 2], 1.0, src[:],
                                                                 ALU.add, ALU.mult))
                    dve.sem_inc(free.sem, 1)
                    dve.sem_inc(s_zused.sem, 1)
                    vec.link(dve, nc.vector.scalar_tensor_tensor(u_a[:, c], silu_z[:], SILU_HALF, u_a[:, c],
                                                                 ALU.mult, ALU.mult))
                    dve.sem_inc(s_ya.sem, 1)
                elif n in JOB_OA:
                    d = n - JOB_OA[0]
                    dve.wait_ge(s_job.sem, s_job.at(layer, n + 1))
                    dve.wait_ge(s_ga.sem, s_ga.at(layer, d + 1))
                    vec.link(dve, nc.vector.scalar_tensor_tensor(g_a[:, d], g_a[:, d], 1.0, src[:], ALU.add, ALU.mult))
                    dve.sem_inc(free.sem, 1)
                    dve.sem_inc(s_ma.sem, 1)
                elif n in JOB_OB:
                    d = n - JOB_OB[0]
                    dve.wait_ge(s_job.sem, s_job.at(layer, n + 1))
                    dve.wait_ge(s_gb.sem, s_gb.at(layer, d + 1))
                    vec.link(dve, nc.vector.scalar_tensor_tensor(g_b[:, d], g_b[:, d], 1.0, src[:], ALU.add, ALU.mult))
                    dve.sem_inc(free.sem, 1)
                    nc.vector.tensor_tensor(g_b[:, d], g_b[:, d], g_a[:, d], ALU.add).then_inc(s_sum.sem, 1)
                    if d:
                        merged_lo(layer, d - 1)
                    if d == KD - 1:
                        merged_lo(layer, d)
                elif n in JOB_OUT:
                    i = n - JOB_OUT[0]
                    t, half = ORDER[i % TILES], i // TILES
                    dve.wait_ge(s_job.sem, s_job.at(layer, n + 1))
                    if i == 0:
                        dve.wait_ge(s_xback.sem, s_xback.at(layer, 16))
                    part = x_sb[:, t, half * W512:(half + 1) * W512]
                    vec.link(dve, nc.vector.tensor_tensor(part, part, src[:], ALU.add))
                    dve.sem_inc(free.sem, 1)
                    dve.sem_inc(s_res.sem, 1)

            def ln_apply(layer, t):
                tile = v_a[:, t]
                vec.link(dve, nc.vector.tensor_scalar(tile, tile, mv[:, t, 0:1], ln_rstd[:, t:t + 1],
                                                      ALU.subtract, ALU.mult))
                vec.link(dve, nc.vector.tensor_tensor(tile, tile, lng_bc[:], ALU.mult))
                nc.vector.tensor_tensor(tile, tile, lnb_bc[:], ALU.add).then_inc(s_ln.sem, 1)

            def beside(layer, n):
                for i in AFTER_IDX.get(n, []):
                    index_add(layer, i)
                if n == JOB_VB[0]:
                    nc.vector.memset(ws_t[CHUNK:P, :, 0:CHUNK], 0.0).then_inc(s_wsz.sem, 1)
                    dve.wait_ge(s_par.sem, s_par.at(layer, 16 * N_PARAMS))
                    nc.vector.tensor_scalar(gate_half[:], gate_raw[:], 0.5, None, ALU.mult).then_inc(s_ghalf.sem, 1)
                if n == JOB_ZB[0]:
                    dve.wait_ge(s_par.sem, s_par.at(layer, 16 * N_PARAMS))
                    dve.wait_ge(s_lnstd.sem, s_lnstd.at(layer, 1))
                    vec.link(dve, nc.vector.reciprocal(ln_rstd[:], ln_std[:]))
                for t in LN_TILES.get(n, []):
                    ln_apply(layer, t)
                for g in AFTER_MIX.get(n, []):
                    dve.wait_ge(s_mix.sem, s_mix.at(layer, g + 1))
                    dve.wait_ge(s_u.sem, s_u.at(layer, TILES))
                    m = bank[3 + g][:].rearrange("p (n i) -> p n i", n=TILES)
                    biased = um[:, 0:SEQ].rearrange("p (n i) -> p n i", n=TILES)
                    vec.link(dve, nc.vector.tensor_tensor(biased, m, bs_bc[:, g].unsqueeze(1).to_broadcast([P, TILES, P]),
                                                          ALU.add))
                    vec.link(dve, nc.vector.tensor_tensor(u_a[:, g], um[:, 0:SEQ], u_a[:, g], ALU.mult))
                    dve.sem_inc(s_um.sem, 1)
                if n - 1 in JOB_ZA:
                    c = n - 1 - JOB_ZA[0]
                    dve.wait_ge(s_yahi.sem, s_yahi.at(layer, c + 1))
                    nc.vector.tensor_tensor(ya_lo[:, c], u_a[:, c], ya_hi[:, c].bitcast(F32), ALU.subtract) \
                        .then_inc(s_yalo.sem, 1)
                if n in AFTER_ATT:
                    i = AFTER_ATT[n]
                    if i < len(ATT_STEPS):
                        attention_max(layer, i)
                    if i >= 2 and ATT_STEPS[i - 2][0] == HEADS - 1:
                        b = ATT_STEPS[i - 2][1]
                        dve.wait_ge(s_pv.sem, s_pv.at(layer, i - 1))
                        y = z_b[:, :, b * P:(b + 1) * P]
                        nc.vector.scalar_tensor_tensor(y, y, SILU_HALF, bank[7][:].rearrange("p (h q) -> p h q", h=HEADS),
                                                       ALU.mult, ALU.mult).then_inc(s_yb.sem, 1)
                    if i < len(ATT_STEPS):
                        attention_scale(layer, i)
                for h in SPLIT_YB.get(n, []):
                    dve.wait_ge(s_ybhi.sem, s_ybhi.at(layer, h + 1))
                    nc.vector.tensor_tensor(yb_lo[:, h], z_b[:, h], yb_hi[:, h].bitcast(F32), ALU.subtract) \
                        .then_inc(s_yblo.sem, 1)

            def x_normalised(layer, t):
                c = 2 * TILES * HEADS + t
                dve.wait_ge(s_xstd.sem, s_xstd.at(layer, t + 1))
                vec.link(dve, nc.vector.reciprocal(rstd[:, c:c + 1], std[:, c:c + 1]))
                if t >= 2:
                    dve.wait_ge(s_xt.sem, s_xt.at(layer, 2 * (t - 1)))
                nc.vector.scalar_tensor_tensor(xn[:, t % 2], x_sb[:, ORDER[t]], rstd[:, c:c + 1], norm_bc[:],
                                               ALU.mult, ALU.mult).then_inc(s_xn.sem, 1)

            def h_remainder(layer, t):
                for half in range(2):
                    dve.wait_ge(s_hhi.sem, s_hhi.at(layer, 2 * t + half + 1))
                    dst = slice(4 * half, 4 * half + 4), slice(ORDER[t] * P, (ORDER[t] + 1) * P)
                    nc.vector.tensor_tensor(h_lo[:, dst[0], dst[1]],
                                            bank[3 + 2 * (t % 2) + half][:].rearrange("p (c q) -> p c q", c=4),
                                            h_hi[:, dst[0], dst[1]].bitcast(F32), ALU.subtract) \
                        .then_inc(s_hlo.sem, 1)

            def first_tile(layer):
                dve.wait_ge(s_norm.sem, s_norm.at(layer, 16))
                x_normalised(layer, 0)

            first_tile(0)
            vec.end_layer(dve)
            with dve.Fori(0, DEPTH) as layer:
                remainder(layer, 0, 0)
                h_remainder(layer, 0)
                remainder(layer, 0, 1)
                dve.wait_ge(s_shi.sem, s_shi.at(layer, 1))
                nc.vector.tensor_tensor(index_lo[:, :, W512:INDEX], s_raw[:], index_hi[:, :, W512:INDEX].bitcast(F32),
                                        ALU.subtract).then_inc(s_slo.sem, 1)
                x_normalised(layer, 1)
                for qt in range(2, NQ):
                    remainder(layer, 0, qt)
                done = {b: 0 for b in range(1, TILES)}

                def topk(n):
                    for b, count in TOPK_SLOTS.get(n, []):
                        pause(dve)
                        for _ in range(count):
                            topk_round(b, done[b])
                            done[b] += 1

                for n in range(NJOBS):
                    if n + 1 < TILES:
                        h_remainder(layer, n + 1)
                    if n + 2 < TILES:
                        x_normalised(layer, n + 2)
                    if n - 1 in AFTER_QI:
                        index_remainder(layer, AFTER_QI[n - 1])
                    for g, qt in quarters_in(n, "vector"):
                        remainder(layer, g, qt)
                    if n >= 1 and n - 1 in JOB_IQ + JOB_K + JOB_Q:
                        rotated(layer, n - 1)
                    if n == NJOBS - 1:
                        first_tile(layer + 1)
                    if n < min(AFTER_ATT):
                        topk(n)
                    evacuate(layer, n)
                    beside(layer, n)
                    if n >= min(AFTER_ATT):
                        topk(n)
                assert all(v == ROUNDS for v in done.values())
                pause(dve)
                vec.end_layer(dve)


def rope_tables(dim):
    inv = (ROPE_THETA ** (-np.arange(0, dim, 2, dtype=np.float64) / dim)).astype(np.float32)
    ang = np.arange(SEQ, dtype=np.float32)[:, None] * inv[None, :]
    cos, sin = np.cos(ang), np.sin(ang)
    lay = lambda a: a.reshape(TILES, P, dim // 2).transpose(1, 0, 2)
    return lay(cos), lay(sin)


def kernel(x, norm_g, w_in, gate_b, a_ln_g, a_ln_b, a_ws, a_bs, q_norm_g, k_norm_g, w_oa, w_ob, w_out):
    import concourse.bacc as bacc
    from concourse.bass_utils import run_bass_kernel_spmd

    gate = np.asarray(gate_b).reshape(DEPTH, 2, KD, P).transpose(0, 3, 1, 2).reshape(DEPTH, P, 2 * KD)
    norm_g = np.concatenate([norm_g, norm_g[:1]])
    arrays = dict(x=np.asarray(x).reshape(SEQ, D), norm_g=norm_g, w_in=w_in, gate_b=gate, a_ln_g=a_ln_g,
                  a_ln_b=a_ln_b, a_ws=a_ws, a_bs=np.asarray(a_bs).reshape(DEPTH, A_GROUPS * P), q_norm_g=q_norm_g,
                  k_norm_g=k_norm_g, w_oa=w_oa, w_ob=w_ob, w_out=w_out, ident=np.eye(P, dtype=np.float32),
                  rope_cs=np.concatenate([*rope_tables(DH), *rope_tables(ID)], axis=2))
    arrays = {k: np.ascontiguousarray(v) for k, v in arrays.items()}
    nc = bacc.Bacc("TRN2", target_bir_lowering=False, num_devices=1)
    aps = {k: nc.dram_tensor(f"in_{k}", v.shape, F32, kind="ExternalInput").ap() for k, v in arrays.items()}
    out = nc.dram_tensor("out", (SEQ, D), F32, kind="ExternalOutput").ap()
    trunk(nc, **aps, out=out)
    r = run_bass_kernel_spmd(nc, [{f"in_{k}": v for k, v in arrays.items()}], core_ids=[0])
    return r.results[0]["out"].reshape(1, SEQ, D)
```
